# Optimizing a Trainium2 kernel written in Bass

```python
import jax, jax.numpy as jnp
from jax import lax
import numpy as np

D_MODEL = 1024
BATCH = 1
SEQ = 256
DEPTH = 2
DEC_BATCH = 1
DEC_SEQ = 32
PAST_LEN = 512

CHUNK = 64
HEAD_DIM = 64
A_HEADS = 4
IDX_HEADS = 8
IDX_DIM = 32
TOPK_MAX = 256
B_GROUPS = 4
B_CHUNK = 128
C_HEADS = 4
D_HEADS = 4
BRANCH_WIDTH = 4 * HEAD_DIM
N_BRANCH = 4
D_FF = 2816
CONV_W = 3
Q_BLOCK = 128
ROPE_THETA = 10000.0
EPS = 1e-6
F_BIAS_INIT = 2.0
IN_SIZES = (A_HEADS * HEAD_DIM, A_HEADS * HEAD_DIM, A_HEADS * HEAD_DIM,
            IDX_HEADS * IDX_DIM, IDX_DIM, IDX_HEADS,
            B_GROUPS * HEAD_DIM, B_GROUPS * HEAD_DIM,
            C_HEADS * HEAD_DIM, C_HEADS * HEAD_DIM, C_HEADS * HEAD_DIM, C_HEADS,
            D_HEADS * HEAD_DIM, D_HEADS * HEAD_DIM, D_HEADS * HEAD_DIM)
IN_COLS = sum(IN_SIZES)

kernel_name = 'hybrid_streaming_encoder_step'

def rms_norm(x, g):
    xf = x.astype(jnp.float32)
    y = xf * lax.rsqrt(jnp.mean(xf * xf, axis=-1, keepdims=True) + EPS)
    return (y * g.astype(jnp.float32)).astype(x.dtype)

def layer_norm(x, g, b):
    xf = x.astype(jnp.float32)
    xc = xf - jnp.mean(xf, axis=-1, keepdims=True)
    var = jnp.mean(xc * xc, axis=-1, keepdims=True)
    return (xc * lax.rsqrt(var + EPS) * g.astype(jnp.float32) + b.astype(jnp.float32)).astype(x.dtype)

def rope(x, pos):
    half = x.shape[-1] // 2
    inv = ROPE_THETA ** (-jnp.arange(half, dtype=jnp.float32) / half)
    ang = pos.astype(jnp.float32)[:, None] * inv[None, :]
    cos = jnp.cos(ang)[:, None, :]
    sin = jnp.sin(ang)[:, None, :]
    xf = x.astype(jnp.float32)
    x1, x2 = xf[..., :half], xf[..., half:]
    return jnp.concatenate([x1 * cos - x2 * sin, x2 * cos + x1 * sin], axis=-1).astype(x.dtype)

def split_cols(p):
    offsets = np.cumsum(np.array(IN_SIZES))[:-1]
    return jnp.split(p, [int(o) for o in offsets], axis=-1)

def to_blocks(a, block):
    b, t = a.shape[:2]
    return jnp.swapaxes(a.reshape(b, t // block, block, *a.shape[2:]), 0, 1)

def from_blocks(a):
    nb, b, blk = a.shape[:3]
    return jnp.swapaxes(a, 0, 1).reshape(b, nb * blk, *a.shape[3:])

def dsa_attend(q, qi, wi, q_pos, k, v, ki, n_sel):
    n_keys = k.shape[1]
    limit = (q_pos // CHUNK + 1) * CHUNK
    dots = jnp.einsum('bqhd,bsd->bqhs', qi.astype(jnp.float32), ki.astype(jnp.float32)) * IDX_DIM ** -0.5
    score = jnp.einsum('bqh,bqhs->bqs', wi.astype(jnp.float32) * IDX_HEADS ** -0.5, jax.nn.relu(dots))
    admissible = jnp.arange(n_keys)[None, :] < limit[:, None]
    score = jnp.where(admissible[None], score, -jnp.inf)
    _, idx = lax.top_k(score, n_sel)
    valid = idx < limit[None, :, None]
    gather = jax.vmap(lambda rows, ids: rows[ids])
    k_sel = gather(k, idx)
    v_sel = gather(v, idx)
    logits = jnp.einsum('bqhd,bqkhd->bhqk', q, k_sel).astype(jnp.float32) * HEAD_DIM ** -0.5
    logits = jnp.where(valid[:, None], logits, -jnp.inf)
    p = jax.nn.softmax(logits, axis=-1).astype(v.dtype)
    return jnp.einsum('bhqk,bqkhd->bqhd', p, v_sel)

def fox_attend(q, f_q, q_pos, k, v, f_k):
    n_keys = k.shape[1]
    s = jnp.einsum('bqhd,bshd->bhqs', q, k).astype(jnp.float32) * HEAD_DIM ** -0.5
    s = s + jnp.moveaxis(f_q, 2, 1)[..., None] - jnp.moveaxis(f_k, 2, 1)[:, :, None, :]
    causal = jnp.arange(n_keys)[None, :] <= q_pos[:, None]
    s = jnp.where(causal, s, -jnp.inf)
    p = jax.nn.softmax(s, axis=-1).astype(v.dtype)
    return jnp.einsum('bhqs,bshd->bqhd', p, v)

def sb_attend(q, q_pos, k, v):
    n_keys = k.shape[1]
    z = jnp.einsum('bqhd,bshd->bhqs', q, k).astype(jnp.float32) * HEAD_DIM ** -0.5
    strict = jnp.arange(n_keys)[None, :] < q_pos[:, None]
    log_keep = jnp.where(strict, jax.nn.log_sigmoid(-z), 0.0)
    later = lax.cumsum(log_keep, axis=3, reverse=True) - log_keep
    weight = jnp.where(strict, jnp.exp(jax.nn.log_sigmoid(z) + later), 0.0)
    return jnp.einsum('bhqs,bshd->bqhd', weight.astype(v.dtype), v)

def spatial_gate(u, v, w_s, b_s):
    n = v.shape[2]
    tri = jnp.tril(jnp.ones((n, n), dtype=bool))
    w = jnp.where(tri[None], w_s[:, :n, :n], 0).astype(v.dtype)
    bias = jnp.swapaxes(b_s[:, :n], 0, 1)[None, None, :, :, None].astype(v.dtype)
    return u * (jnp.einsum('gts,bnsgc->bntgc', w, v) + bias)

def token_mixers(h, w_in, f_bias, lnv_g, lnv_b, w_s, b_s, w_branch, w_gate, b_gate, w_out, past):
    B, T, _ = h.shape
    (a_q, a_k, a_v, a_qi, a_ki, a_w, b_u, b_v,
     c_q, c_k, c_v, c_f, d_q, d_k, d_v) = split_cols(h @ w_in)
    heads = lambda t: t.reshape(B, T, -1, HEAD_DIM)
    past_len = 0 if past is None else past[0].shape[1]
    pos = past_len + jnp.arange(T)
    q_a, k_a, v_a = rope(heads(a_q), pos), rope(heads(a_k), pos), heads(a_v)
    qi = rope(a_qi.reshape(B, T, IDX_HEADS, IDX_DIM), pos)
    ki = rope(a_ki[:, :, None, :], pos)[:, :, 0, :]
    u = jax.nn.gelu(b_u)
    v_b = layer_norm(jax.nn.gelu(b_v), lnv_g, lnv_b)
    n = min(T, B_CHUNK)
    o_b = spatial_gate(u.reshape(B, T // n, n, B_GROUPS, HEAD_DIM),
                       v_b.reshape(B, T // n, n, B_GROUPS, HEAD_DIM), w_s, b_s).reshape(B, T, BRANCH_WIDTH)
    q_c, k_c, v_c = heads(c_q), heads(c_k), heads(c_v)
    logf = jax.nn.log_sigmoid(c_f.astype(jnp.float32) + f_bias.astype(jnp.float32))
    q_d, k_d, v_d = heads(d_q), heads(d_k), heads(d_v)
    if past is None:
        n_sel = min(TOPK_MAX, T // 4)
        o_a = from_blocks(lax.map(
            lambda blk: dsa_attend(blk[0], blk[1], blk[2], blk[3], k_a, v_a, ki, n_sel),
            (to_blocks(q_a, CHUNK), to_blocks(qi, CHUNK), to_blocks(a_w, CHUNK), pos.reshape(-1, CHUNK))))
        f_all = lax.cumsum(logf, axis=1)
        o_c = from_blocks(lax.map(
            lambda blk: fox_attend(blk[0], blk[1], blk[2], k_c, v_c, f_all),
            (to_blocks(q_c, Q_BLOCK), to_blocks(f_all, Q_BLOCK), pos.reshape(-1, Q_BLOCK))))
        o_d = from_blocks(lax.map(
            lambda blk: sb_attend(blk[0], blk[1], k_d, v_d),
            (to_blocks(q_d, Q_BLOCK), pos.reshape(-1, Q_BLOCK))))
    else:
        (pk_a, pv_a, pki, pk_c, pv_c, plogf, pk_d, pv_d) = past
        cat = lambda old, new: jnp.concatenate([old, new], axis=1)
        n_sel = min(TOPK_MAX, (past_len + T) // 4)
        o_a = dsa_attend(q_a, qi, a_w, pos, cat(pk_a, k_a), cat(pv_a, v_a), cat(pki, ki), n_sel)
        f_all = lax.cumsum(cat(plogf.astype(jnp.float32), logf), axis=1)
        o_c = fox_attend(q_c, f_all[:, past_len:], pos, cat(pk_c, k_c), cat(pv_c, v_c), f_all)
        o_d = sb_attend(q_d, pos, cat(pk_d, k_d), cat(pv_d, v_d))
    branches = (o_a.reshape(B, T, -1), o_b, o_c.reshape(B, T, -1), o_d.reshape(B, T, -1))
    gates = jax.nn.sigmoid((h @ w_gate + b_gate).astype(jnp.float32)).astype(h.dtype)
    gates = gates.reshape(B, T, N_BRANCH, D_MODEL)
    merged = gates[:, :, 0] * (branches[0] @ w_branch[0])
    for i in range(1, N_BRANCH):
        merged = merged + gates[:, :, i] * (branches[i] @ w_branch[i])
    return merged @ w_out, (k_a, v_a, ki, v_b, k_c, v_c, logf, k_d, v_d)

def conv_ffn(h, w_up, w_conv, b_conv, w_down, prefix):
    T = h.shape[1]
    up = h @ w_up
    ext = jnp.concatenate([prefix.astype(up.dtype), up], axis=1)
    conv = ext[:, 0:T] * w_conv[0]
    for j in range(1, CONV_W):
        conv = conv + ext[:, j:j + T] * w_conv[j]
    conv = conv + b_conv
    gate, val = jnp.split(conv, 2, axis=-1)
    return (jax.nn.silu(gate) * val) @ w_down, ext[:, T:]

def trunk_layer(x, c, params, past, conv_prefix):
    (g1, g2, w_mod, b_mod, w_in, f_bias, lnv_g, lnv_b, w_s, b_s,
     w_branch, w_gate, b_gate, w_out, w_up, w_conv, b_conv, w_down) = params
    mod = jax.nn.silu(c) @ w_mod + b_mod
    shift1, scale1, gate1, shift2, scale2, gate2 = [m[:, None, :] for m in jnp.split(mod, 6, axis=-1)]
    h = rms_norm(x, g1) * (1 + scale1) + shift1
    y, rows = token_mixers(h, w_in, f_bias, lnv_g, lnv_b, w_s, b_s, w_branch, w_gate, b_gate, w_out, past)
    x = x + gate1 * y
    h = rms_norm(x, g2) * (1 + scale2) + shift2
    f, conv_state = conv_ffn(h, w_up, w_conv, b_conv, w_down, conv_prefix)
    x = x + gate2 * f
    return x, rows + (conv_state,)

def setup_inputs(seed: int = 0) -> dict:
    key = jax.random.key(seed)
    ks = iter(jax.random.split(key, 40))
    nrm = lambda shape, scale=1.0: scale * jax.random.normal(next(ks), shape, jnp.float32)
    kv = lambda h: (DEPTH, DEC_BATCH, PAST_LEN, h, HEAD_DIM)
    return {
        'x_prompt': nrm((BATCH, SEQ, D_MODEL)),
        'x_sample': nrm((DEC_BATCH, DEC_SEQ, D_MODEL)),
        'cache_a_k': nrm(kv(A_HEADS)),
        'cache_a_v': nrm(kv(A_HEADS)),
        'cache_a_kidx': nrm((DEPTH, DEC_BATCH, PAST_LEN, IDX_DIM)),
        'cache_c_k': nrm(kv(C_HEADS)),
        'cache_c_v': nrm(kv(C_HEADS)),
        'cache_c_logf': jax.nn.log_sigmoid(nrm((DEPTH, DEC_BATCH, PAST_LEN, C_HEADS)) + F_BIAS_INIT),
        'cache_d_k': nrm(kv(D_HEADS)),
        'cache_d_v': nrm(kv(D_HEADS)),
        'state_ffn_conv': nrm((DEPTH, DEC_BATCH, CONV_W - 1, 2 * D_FF)),
        'c_prompt': nrm((BATCH, D_MODEL)),
        'c_sample': nrm((DEC_BATCH, D_MODEL)),
        'norm1_g': 1.0 + nrm((DEPTH, D_MODEL), 0.05),
        'norm2_g': 1.0 + nrm((DEPTH, D_MODEL), 0.05),
        'w_mod': nrm((DEPTH, D_MODEL, 6 * D_MODEL), 0.5 * D_MODEL ** -0.5),
        'b_mod': nrm((DEPTH, 6 * D_MODEL), 0.02),
        'w_in': nrm((DEPTH, D_MODEL, IN_COLS), D_MODEL ** -0.5),
        'f_bias': F_BIAS_INIT + nrm((DEPTH, C_HEADS), 0.5),
        'lnv_g': 1.0 + nrm((DEPTH, BRANCH_WIDTH), 0.05),
        'lnv_b': nrm((DEPTH, BRANCH_WIDTH), 0.02),
        'w_spatial': nrm((DEPTH, B_GROUPS, B_CHUNK, B_CHUNK), B_CHUNK ** -0.5),
        'b_spatial': 1.0 + nrm((DEPTH, B_GROUPS, B_CHUNK), 0.1),
        'w_branch': nrm((DEPTH, N_BRANCH, BRANCH_WIDTH, D_MODEL), BRANCH_WIDTH ** -0.5),
        'w_gate': nrm((DEPTH, D_MODEL, N_BRANCH * D_MODEL), D_MODEL ** -0.5),
        'b_gate': nrm((DEPTH, N_BRANCH * D_MODEL), 0.02),
        'w_out': nrm((DEPTH, D_MODEL, D_MODEL), D_MODEL ** -0.5),
        'w_up': nrm((DEPTH, D_MODEL, 2 * D_FF), D_MODEL ** -0.5),
        'w_conv': nrm((DEPTH, CONV_W, 2 * D_FF), CONV_W ** -0.5),
        'b_conv': nrm((DEPTH, 2 * D_FF), 0.02),
        'w_down': nrm((DEPTH, D_FF, D_MODEL), D_FF ** -0.5),
        'final_g': 1.0 + nrm((D_MODEL,), 0.05),
    }

def reference(x_prompt, x_sample, cache_a_k, cache_a_v, cache_a_kidx, cache_c_k, cache_c_v, cache_c_logf,
              cache_d_k, cache_d_v, state_ffn_conv, c_prompt, c_sample, norm1_g, norm2_g, w_mod, b_mod, w_in,
              f_bias, lnv_g, lnv_b, w_spatial, b_spatial, w_branch, w_gate, b_gate, w_out, w_up, w_conv, b_conv,
              w_down, final_g):
    prefix = jnp.zeros((x_prompt.shape[0], CONV_W - 1, w_up.shape[-1]), x_prompt.dtype)
    xp, xs = x_prompt, x_sample
    rows_p, rows_s = [], []
    for l in range(DEPTH):
        params = (norm1_g[l], norm2_g[l], w_mod[l], b_mod[l], w_in[l], f_bias[l], lnv_g[l], lnv_b[l],
                  w_spatial[l], b_spatial[l], w_branch[l], w_gate[l], b_gate[l], w_out[l], w_up[l],
                  w_conv[l], b_conv[l], w_down[l])
        past = (cache_a_k[l], cache_a_v[l], cache_a_kidx[l], cache_c_k[l], cache_c_v[l], cache_c_logf[l],
                cache_d_k[l], cache_d_v[l])
        xp, new_p = trunk_layer(xp, c_prompt, params, None, prefix)
        xs, new_s = trunk_layer(xs, c_sample, params, past, state_ffn_conv[l])
        rows_p.append(new_p)
        rows_s.append(new_s)

    def stacked(rows, i):
        return jnp.stack([r[i] for r in rows], axis=0)

    y_prompt = rms_norm(xp, final_g)
    y_sample = rms_norm(xs, final_g)
    return (y_prompt, y_sample,
            stacked(rows_p, 0), stacked(rows_s, 0),
            stacked(rows_p, 1), stacked(rows_s, 1),
            stacked(rows_p, 2), stacked(rows_s, 2),
            stacked(rows_s, 3),
            stacked(rows_p, 4), stacked(rows_s, 4),
            stacked(rows_p, 5), stacked(rows_s, 5),
            stacked(rows_p, 6), stacked(rows_s, 6),
            stacked(rows_p, 7), stacked(rows_s, 7),
            stacked(rows_p, 8), stacked(rows_s, 8),
            stacked(rows_p, 9), stacked(rows_s, 9))


_drawn_inputs = setup_inputs


def setup_inputs(seed=0):
    import zlib

    import numpy as np

    out = dict(_drawn_inputs(seed))
    spreads = {}
    factors = {'cache_c_logf': 35.159,
     'cache_d_k': 3.746,
     'lnv_b': 2.939,
     'b_spatial': 3.341,
     'b_gate': 8.0,
     'b_conv': 6.968,
     'cache_c_k': 2.951}
    for name, (base, spread) in spreads.items():
        noise = np.random.default_rng([zlib.crc32(name.encode()), seed]).standard_normal(out[name].shape)
        drawn = base * np.exp(spread * noise) if base else spread * noise
        out[name] = __import__('jax').numpy.asarray(drawn.astype(out[name].dtype))
    for name, factor in factors.items():
        out[name] = (out[name] * factor).astype(out[name].dtype)
    return out
```

```python
from contextlib import ExitStack

import concourse.bass as bass
from concourse import mybir

F32 = mybir.dt.float32
F32R = mybir.dt.float32r
ALU = mybir.AluOpType
ACT = mybir.ActivationFunctionType
X = mybir.AxisListType.X

P = 128
DM = 1024
DEPTH = 2
TP, TS = 256, 32
T = TP + TS
PAST = 512
HD = 64
NH = 4
IH = 8
IDX = 32
FF = 2816
KT = DM // P
FT = FF // P
SEL_P = (TP // 4) // 8
SEL_S = ((PAST + TS) // 4) // 8
EPS = 1e-6
MASKED = -1e30
INADMISSIBLE = -1e38
TAKEN = -3e38

AQ, AK, AV, AQI, BU, BV, CQ, CK, CV, DQ, DK, DV, AKI, MISC = 0, 2, 4, 6, 8, 10, 12, 14, 16, 18, 20, 22, 24, 25
NIN = 26
FROW, WROW = 0, 32

PIECE = 1024
NMOD = 48
MOD_A = 16
MOD_BLOCKS = NMOD // 4
FIRST_BLOCKS = MOD_A // 4
Q_IN, Q_GATE, Q_BRANCH, Q_OUT, Q_UP = 0, 26, 58, 66, 74
Q_DOWN = Q_UP + 2 * FT
DOWN_SPLIT = (8, 7, 7)
NSPLIT = Q_DOWN + KT * 3
NPIECE = NMOD + NSPLIT
RING = 4
AHEAD = 3

C_ID, C_PA, C_PI, C_ADM, C_CAUSAL, C_STRICT, C_STRICT1, C_SPAT, C_NTRI, C_NONE, C_ONE, C_REP = (P * i for i in range(12))
C_COSA = 12 * P
C_SINA, C_COSI, C_SINI = C_COSA + T, C_COSA + 2 * T, C_COSA + 3 * T
C_NEW = C_COSA + 4 * T
C_QS = C_NEW + TS
C_EPS = C_QS + NIN
C_FR = C_EPS + 1
C_FL = C_FR + 2
C_HALF = C_FL + 2 * NH
NCONST = C_HALF + 2

V_LG, V_LB = 0, 2
V_GATE = 4
V_CONV = V_GATE + 32
V_CB = V_CONV + 3 * 2 * FT
V_ST = V_CB + 2 * FT
V_FB = V_ST + 4 * FT
V_BS = V_FB + 1
NVEC = V_BS + 2 * P

M_MOD, M_G1, M_G2, NMV = 0, NMOD, NMOD + KT, NMOD + 2 * KT

N_PROJ_STORES = 10
UC = T + 4
CC = T + 2


def encoder(nc, x_fm, mod_first, mod_vecs, c_fm, stream, vecs, consts, final_g, keys_t, vals, kidx_t, logf_past, w_sp_t,
            y_fm, o_proj, o_ki, o_vb, o_logf, o_conv):
    with ExitStack() as ctx:
        top = [0]

        def place(name, shape, dt, at=None):
            size = 4
            for n in shape[1:]:
                size *= n
            size = (size + 31) // 32 * 32
            off = top[0] if at is None else at
            if at is None:
                top[0] = off + size
                assert top[0] <= 224 * 1024 - 64, (name, top[0])
            return nc.alloc_sbuf_tensor_at(name, shape, dt, offset=off), off, size

        base = (nc.sbuf_base + 31) // 32 * 32
        top[0] = base

        raw, _, _ = place("raw", [P, RING, PIECE], F32)
        whi, _, _ = place("whi", [P, RING, PIECE], F32R)
        wlo, _, _ = place("wlo", [P, RING, PIECE], F32R)
        cst, _, _ = place("cst", [P, NCONST], F32)
        vec, _, _ = place("vec", [P, NVEC], F32)
        x, _, _ = place("x", [P, KT, T], F32)
        work, work_at, _ = place("work", [P, KT, T], F32)
        hh, _, _ = place("hh", [P, KT, T], F32R)
        hl, _, _ = place("hl", [P, KT, T], F32R)
        oh, _, _ = place("oh", [P, KT, T], F32R)
        ol, _, _ = place("ol", [P, KT, T], F32R)
        proj, proj_at, proj_n = place("proj", [P, NIN, T], F32)
        gates, gates_at, gates_n = place("gates", [P, 4 * KT, T], F32)
        kv0k, kv0_at, _ = place("kv0k", [P, 2, PAST], F32)
        kv0v, _, _ = place("kv0v", [P, 4, 2 * P], F32)
        kv1k, _, _ = place("kv1k", [P, 2, PAST], F32)
        kv1v, _, _ = place("kv1v", [P, 4, 2 * P], F32)
        kix, _, _ = place("kix", [P, PAST], F32)
        wsp, _, _ = place("wsp", [P, 4, P], F32)
        fah, _, n = place("fah", [P, FT, CC], F32R, at=proj_at)
        fal, _, n2 = place("fal", [P, FT, CC], F32R, at=proj_at + n)
        assert n + n2 <= gates_at + gates_n - proj_at
        probs, _, n = place("probs", [P, 1024], F32, at=work_at)
        probs_t, _, n2 = place("probs_t", [P, 8, P], F32, at=work_at + n)
        at = [gates_at]

        def scratch(name, shape):
            t, _, n = place(name, shape, F32, at=at[0])
            at[0] += n
            assert at[0] <= gates_at + gates_n, name
            return t

        d_keep = scratch("d_keep", [P, 2, 512])
        d_wt = scratch("d_wt", [P, 2, 512])
        vt = scratch("vt", [P, 3, 2 * P])
        scr = scratch("scr", [P, 2, 2 * T])
        queries = scr[:].rearrange("p a (b n) -> p (a b) n", b=2)
        score = scratch("score", [P, 3 * P + PAST + TS])
        fl8 = scratch("fl8", [8, NH, T])
        fcum_all = scratch("fcum", [P, TP + PAST + TS])
        fr_all = scratch("fr8", [P, TP + PAST + TS])
        fcum, fr8 = fcum_all[0:8], fr_all[0:8]
        mod_rows = [t[32:34, 0:512] for t in (fcum_all, fr_all)]
        lfp = scratch("lfp", [8, PAST])
        up, _, n = place("up", [P, 4, UC], F32, at=kv0_at)
        conv, _, n2 = place("conv", [P, 4, CC], F32, at=kv0_at + n)
        sil, _, n3 = place("sil", [P, 2, CC], F32, at=kv0_at + n + n2)
        prod, _, _ = place("prod", [P, 2, CC], F32, at=kv0_at + n + n2 + n3)

        lf, _, _ = place("lf", [8, T], F32)
        small, _, _ = place("small", [P, 64], F32)
        cmod, _, _ = place("cmod", [P, KT, 4], F32)
        mod, _, _ = place("mod", [P, NMOD, 2], F32)
        mvec, _, _ = place("mvec", [P, (DEPTH + 1) * NMV], F32)
        norm_a, _, _ = place("norm_a", [P, 2, KT, 2], F32)
        d_new, _, _ = place("d_new", [TS, 2, P], F32)
        tail, _, _ = place("tail", [P, 2 * FT, 4], F32)
        fg, _, _ = place("fg", [P, KT], F32)
        rstd, _, _ = place("rstd", [P, 2, T], F32)
        ctx.enter_context(nc.sbuf_tensor("fence", [P, top[0] - base + 64], mybir.dt.uint8))

        ps = ctx.enter_context(nc.psum_tensor("ps", [P, 8, 512], F32))
        flat = ps[:].rearrange("p b n -> p (b n)")

        def sem(name):
            return ctx.enter_context(nc.semaphore(name))

        per_layer = {}

        def signal(name, n):
            per_layer[name] = n
            return sem(name)

        raw_loaded = [sem(f"raw_loaded{s}") for s in range(RING)]
        raw_per_layer = [len(range(s, NPIECE, RING)) for s in range(RING)]
        bank_free = [sem(f"bank_free{b}") for b in range(2)]
        TILES2 = (NIN + 10 * KT) // 2
        start_loaded = sem("start_loaded")
        y_stored = sem("y_stored")
        vecs_loaded = signal("vecs_loaded", 3 * 16)
        kv_d_loaded = signal("kv_d_loaded", 3 * 16)
        kv_c_loaded = signal("kv_c_loaded", 2 * 16)
        kv_a_loaded = signal("kv_a_loaded", 2 * 16)
        proj_stored = signal("proj_stored", N_PROJ_STORES * 16)
        tail_stored = signal("tail_stored", 16)
        mod_read = signal("mod_read", NMOD)
        hi_ready = signal("hi_ready", NSPLIT)
        lo_ready = signal("lo_ready", NSPLIT)
        piece_done = signal("piece_done", NSPLIT + 24)
        rows_taken = signal("rows_taken", MOD_BLOCKS)
        rows_turned = signal("rows_turned", MOD_BLOCKS)
        mod_ready = signal("mod_ready", MOD_BLOCKS)
        squared = signal("squared", 2)
        sums_ready = signal("sums_ready", 2)
        rstd_guess = signal("rstd_guess", 2)
        h_scaled = signal("h_scaled", 2)
        hh_ready = signal("hh_ready", 2)
        hl_ready = signal("hl_ready", 2)
        swapped = signal("swapped", 7)
        swap_read = signal("swap_read", 7)
        roped = signal("roped", 7)
        w_turned = signal("w_turned", 1)
        w_read = signal("w_read", 1)
        gelued = signal("gelued", 1)
        mean_ready = signal("mean_ready", 1)
        centred = signal("centred", 1)
        centred_squared = signal("centred_squared", 1)
        var_ready = signal("var_ready", 1)
        b_guess = signal("b_guess", 1)
        vb_ready = signal("vb_ready", 1)
        vb_turned = signal("vb_turned", 1)
        vb_tok = signal("vb_tok", 1)
        spatial_masked = signal("spatial_masked", 1)
        spatial_ready = signal("spatial_ready", 1)
        b_summed = signal("b_summed", 2)
        v_turned = signal("v_turned", 3)
        v_tok = signal("v_tok", 3)
        znew_ready = signal("znew_ready", 1)
        znew_log = signal("znew_log", 1)
        znew_keep = signal("znew_keep", 1)
        znew_logw = signal("znew_logw", 1)
        wnew_ready = signal("wnew_ready", 1)
        z_ready = signal("z_ready", NH)
        z_log = signal("z_log", NH)
        keep_ready = signal("keep_ready", NH)
        logw_ready = signal("logw_ready", NH)
        wt_ready = signal("wt_ready", NH)
        d_out = signal("d_out", NH)
        oh_ready = signal("oh_ready", 8)
        ol_ready = signal("ol_ready", 8)
        f_ready = signal("f_ready", 1)
        f_log = signal("f_log", 1)
        queries_ready = signal("queries_ready", 2)
        logits = signal("logits", 6)
        max_ready = signal("max_ready", 6)
        exp_ready = signal("exp_ready", 6)
        probs_ready = signal("probs_ready", 6)
        turned = signal("turned", 6)
        probs_tok = signal("probs_tok", 6)
        pv_done = signal("pv_done", 6)
        dots = signal("dots", 3 * IH)
        relued = signal("relued", 3 * IH)
        scored = signal("scored", 3 * IH)
        chosen = signal("chosen", 3)
        sigmoid_ready = signal("sigmoid_ready", 4)
        merged = signal("merged", 1)
        merged_h = signal("merged_h", 1)
        merged_l = signal("merged_l", 1)
        up_copied = signal("up_copied", 2 * FT)
        convolved = signal("convolved", 2 * FT)
        silued = signal("silued", FT)
        product_ready = signal("product_ready", FT)
        fah_ready = signal("fah_ready", FT)
        fal_ready = signal("fal_ready", FT)
        c_ready, c_exp, c_sig = sem("c_ready"), sem("c_exp"), sem("c_sig")
        y_ready = sem("y_ready")
        fin = [sem(f"final{i}") for i in range(6)]

        start_at = {"lo_ready": 1, "piece_done": 1, "tail_stored": 1}
        start_at.update(mod_read=MOD_A, rows_taken=FIRST_BLOCKS, rows_turned=FIRST_BLOCKS,
                        mod_ready=FIRST_BLOCKS)
        settled = sem("settled")

        def upto(l, signal, k=None):
            n = per_layer[signal.name]
            return l * n + ((n if k is None else k) + start_at.get(signal.name, 0))

        def taken(l, tiles):
            return l * TILES2 + (tiles + 1)

        def loaded(l, slot, piece, more=0):
            return l * (16 * raw_per_layer[slot]) + (more + 16 * (MOD_A // RING + piece // RING + 1))

        def place_of(q):
            return q if q < NIN else q + NMOD

        ACT_LINKS, DVE_LINKS = LINKS
        act_own, dve_own = sem("act_own"), sem("dve_own")

        def done(q, j=0):
            if q < Q_BRANCH:
                return q + 1
            if q < Q_OUT:
                return Q_BRANCH + 4 * (q - Q_BRANCH) + j + 1
            return q + 1 + 24

        znew = ps[0:TS, 6:8, 0:2 * TS]

        def new_at(h):
            return (h % 2) * 2 * TS + (h // 2) * TS

        block = ctx.enter_context(nc.Block())

        @block.sync
        def _(sp):
            sp.dma_start(cst[:], consts).then_inc(start_loaded, 16)
            sp.dma_start(x[:], x_fm).then_inc(start_loaded, 16)
            sp.dma_start(cmod[:, :, 0:2], c_fm).then_inc(start_loaded, 16)
            sp.dma_start(fg[:], final_g).then_inc(start_loaded, 16)
            rounds = stream.rearrange("l (r s) p n -> l r s p n", s=2)
            sp.dma_start(mvec[:], mod_vecs).then_inc(start_loaded, 16)
            for i in range(MOD_A):
                if i >= RING:
                    sp.wait_ge(mod_read, i - RING + 1)
                sp.dma_start(raw[:, i % RING, :], mod_first[i]).then_inc(raw_loaded[i % RING], 16)
            with sp.Fori(0, DEPTH) as l:
                def load(pair, slot):
                    for j in range(2):
                        sp.dma_start(raw[:, slot + j, :], rounds[l, pair, j]).then_inc(raw_loaded[slot + j], 16)

                sp.wait_ge(mod_read, upto(l, mod_read, 0))
                for i in range(2):
                    sp.wait_ge(lo_ready, upto(l, lo_ready, 0))
                    load(i, 2 * i)
                sp.wait_ge(bank_free[0], taken(l, 0))
                sp.wait_ge(bank_free[1], taken(l, 0))
                sp.wait_ge(mod_ready, upto(l, mod_ready, 0))
                sp.dma_start(vec[:], vecs[l]).then_inc(vecs_loaded, 16)
                sp.dma_start(wsp[:], w_sp_t[l]).then_inc(vecs_loaded, 16)
                sp.dma_start(lfp[:], logf_past[l]).then_inc(vecs_loaded, 16)

                def split_pair(pair, at):
                    sp.wait_ge(lo_ready, upto(l, lo_ready, 2 * pair - 2))
                    load(at // 2 + pair, 2 * (pair % 2))

                def split_rounds(a, b, at):
                    with sp.Fori(0, (b - a) // 2) as r:
                        for i in range(2):
                            sp.wait_ge(lo_ready, upto(l, lo_ready, r * 4 + 2 * (a + i) - 2))
                            load(r * 2 + at // 2 + a + i, 2 * ((a + i) % 2))

                split_rounds(2, 4, 0)
                sp.dma_start(kv0k[:], keys_t[l, 2]).then_inc(kv_d_loaded, 16)
                sp.dma_start(kv0v[:], vals[l, 2]).then_inc(kv_d_loaded, 16)
                sp.dma_start(kix[:], kidx_t[l]).then_inc(kv_d_loaded, 16)
                sp.dma_start(kv1k[:], keys_t[l, 1]).then_inc(kv_c_loaded, 16)
                sp.dma_start(kv1v[:], vals[l, 1]).then_inc(kv_c_loaded, 16)
                split_rounds(4, 12, 0)
                split_pair(12, 0)
                for i in range(2):
                    sp.wait_ge(lo_ready, upto(l, lo_ready, NIN - 2 + 2 * i))
                    load(NIN // 2 + i, 2 * (1 - i))

                def mod_rounds(a, b):
                    with sp.Fori(0, (b - a) // 2) as r:
                        for i in range(2):
                            sp.wait_ge(mod_read, upto(l, mod_read, r * 4 + 2 * (a + i) - 2))
                            load(r * 2 + NIN // 2 + a + i, 2 * (1 - i))

                mod_rounds(2, 12)
                sp.wait_ge(d_out, upto(l, d_out))
                sp.sem_inc(settled, 1)
                sp.dma_start(kv0k[:], keys_t[l, 0]).then_inc(kv_a_loaded, 16)
                sp.dma_start(kv0v[:], vals[l, 0]).then_inc(kv_a_loaded, 16)
                mod_rounds(12, NMOD // 2)
                for i in range(2):
                    sp.wait_ge(mod_read, upto(l, mod_read, NMOD - 2 + 2 * i))
                    load((NIN + NMOD) // 2 + i, 2 * (1 - i))
                split_rounds(NIN // 2 + 2, 35, NMOD)
                sp.wait_ge(bank_free[0], taken(l, (NIN) // 2))
                sp.wait_ge(bank_free[1], taken(l, (NIN) // 2))
                sp.wait_ge(roped, upto(l, roped))
                sp.sem_inc(settled, 1)
                sp.wait_ge(vb_ready, upto(l, vb_ready))
                sp.wait_ge(f_ready, upto(l, f_ready))
                for i, t in enumerate((AK, AV, CK, CV, DK, DV)):
                    sp.dma_start(o_proj[l, i], proj[:, t:t + 2, :]).then_inc(proj_stored, 16)
                sp.dma_start(o_ki[l], proj[0:IDX, AKI, :]).then_inc(proj_stored, 16)
                sp.dma_start(o_vb[l, 0], proj[:, BV, TP:T]).then_inc(proj_stored, 16)
                sp.dma_start(o_vb[l, 1], proj[:, BV + 1, TP:T]).then_inc(proj_stored, 16)
                sp.dma_start(o_logf[l], lf[0:NH, :]).then_inc(proj_stored, 16)
                split_rounds(35, NSPLIT // 2, NMOD)
                sp.wait_ge(convolved, upto(l, convolved))
                sp.dma_start(o_conv[l], tail[:]).then_inc(tail_stored, 16)
            sp.wait_ge(y_ready, 1)
            sp.dma_start(y_fm, work[:]).then_inc(y_stored, 16)
            sp.wait_ge(y_stored, 16)
            sp.wait_ge(proj_stored, DEPTH * 16 * N_PROJ_STORES)
            sp.wait_ge(tail_stored, DEPTH * 16 + 1)

        @block.gpsimd
        def _(pool):
            for s in (*bank_free, lo_ready, piece_done, tail_stored):
                pool.sem_inc(s, 1)
            with pool.Fori(0, DEPTH) as l:
                def low(slot, q):
                    pool.wait_ge(hi_ready, upto(l, hi_ready, q + 1))
                    nc.gpsimd.tensor_tensor(wlo[:, slot, :], raw[:, slot, :], whi[:, slot, :].bitcast(F32),
                                                  ALU.subtract).then_inc(lo_ready, 1)

                with pool.Fori(0, NSPLIT // RING) as r:
                    for s in range(RING):
                        low(s, r * RING + s)
                for s in range(NSPLIT % RING):
                    low(s, NSPLIT - NSPLIT % RING + s)

        @block.tensor
        def _(pe):
            mm = nc.tensor.matmul
            ident = cst[:, C_ID:C_ID + P]

            def turn(out, in_):
                k = in_.shape[0]
                return mm(out, in_, ident[0:k, 0:k], start=True, stop=True, is_transpose=True)

            def mod_block(l, j):
                bank = j % 2
                if l is not None or j >= 2:
                    pe.wait_ge(mod_ready, j - 1 if l is None else upto(l, mod_ready, j - 1))
                for n in range(4):
                    slot = n if l is None else (NIN + n) % RING
                    pe.wait_ge(raw_loaded[slot], 16 * (j + 1) if l is None else loaded(l, slot, NIN + 4 * j + n))
                    for k in range(2):
                        i = mm(ps[32:34, bank, :], cmod[:, 2 * n + k, 2:4], raw[:, slot, k * 512:(k + 1) * 512],
                               start=(n + k == 0), stop=(n + k == 4))
                    i.then_inc(mod_read, 1)

            def mod_turn(l, j):
                pe.wait_ge(rows_taken, j + 1 if l is None else upto(l, rows_taken, j + 1))
                for m in range(4):
                    i = mm(ps[:, j % 2, 2 * m:2 * m + 2], mod_rows[j % 2][:, m * P:(m + 1) * P], ident[32:34, 32:34],
                           start=True, stop=True)
                i.then_inc(rows_turned, 1)

            def mod_step(l, j, blocks):
                if j < blocks:
                    mod_block(l, j)
                if 0 < j <= blocks:
                    mod_turn(l, j - 1)

            pe.wait_ge(c_sig, 1)
            pe.wait_ge(start_loaded, 80)
            for j in range(FIRST_BLOCKS + 1):
                mod_step(None, j, FIRST_BLOCKS)
            with pe.Fori(0, DEPTH) as l:
                def sums(n):
                    pe.wait_ge(squared, upto(l, squared, n))
                    for k in range(KT):
                        i = mm(ps[:, 7, 0:T], cst[:, C_ONE:C_ONE + P], work[:, k, :], start=(k == 0), stop=(k == KT - 1))
                    i.then_inc(sums_ready, 1)

                def product(out, slot, wcols, terms):
                    n = len(terms)
                    for i, (k, high, low) in enumerate(terms):
                        a, b = k * P * wcols[0] + wcols[1] * P, k * P * wcols[0] + wcols[1] * P + P
                        mm(out, whi[:, slot, a:b], high, start=(i == 0 and wcols[2]), stop=False)
                        mm(out, whi[:, slot, a:b], low, start=False, stop=False)
                        last = mm(out, wlo[:, slot, a:b], high, start=False, stop=(i == n - 1 and wcols[3]))
                    return last

                h_terms = [(k, hh[:, k, :], hl[:, k, :]) for k in range(KT)]

                def tile_piece(slot, q, bank, tile2):
                    pe.wait_ge(lo_ready, upto(l, lo_ready, q + 1))
                    pe.wait_ge(bank_free[bank], taken(l, tile2))
                    product(ps[:, bank, 0:T], slot, (1, 0, True, True), h_terms).then_inc(piece_done, 1)

                def tiles(q0, n, tile0):
                    s0 = q0 % RING
                    if n >= RING:
                        with pe.Fori(0, n // RING) as r:
                            for j in range(RING):
                                tile_piece((s0 + j) % RING, r * RING + q0 + j, j % 2, r * 2 + (tile0 + j) // 2)
                    for j in range(n - n % RING, n):
                        tile_piece((s0 + j) % RING, q0 + j, j % 2, (tile0 + j) // 2)

                sums(1)
                pe.wait_ge(hl_ready, upto(l, hl_ready, 1))
                pe.wait_ge(mod_ready, upto(l, mod_ready, 0))
                pe.sem_inc(settled, 1)
                tiles(Q_IN, NIN, 0)

                pe.wait_ge(bank_free[0], taken(l, (NIN) // 2))
                pe.wait_ge(bank_free[1], taken(l, (NIN) // 2))
                for n, t in enumerate((AQ, AQ + 1, AK, AK + 1, AQI, AQI + 1, AKI)):
                    if n >= 2:
                        pe.wait_ge(swap_read, upto(l, swap_read, n - 1))
                    perm = C_PA if n < 4 else C_PI
                    mm(ps[:, 4 + n % 2, 0:T], cst[:, perm:perm + P], proj[:, t, :], start=True, stop=True).then_inc(swapped, 1)
                for b, (a, n) in enumerate(((0, P), (P, P), (TP, TS))):
                    i = mm(ps[0:n, 7, 8 * b:8 * b + IH], proj[WROW:WROW + IH, MISC, a:a + n],
                           ident[WROW:WROW + IH, WROW:WROW + IH], start=True, stop=True)
                i.then_inc(w_turned, 1)

                mod_step(l, 0, MOD_BLOCKS)
                pe.wait_ge(gelued, upto(l, gelued))
                pe.wait_ge(w_read, upto(l, w_read))
                for j in range(2):
                    i = mm(ps[:, 7, 0:T], cst[:, C_ONE:C_ONE + P], proj[:, BV + j, :], start=(j == 0), stop=(j == 1))
                i.then_inc(mean_ready, 1)
                pe.wait_ge(centred_squared, upto(l, centred_squared))
                for j in range(2):
                    i = mm(ps[:, 7, 0:T], cst[:, C_ONE:C_ONE + P], scr[:, j, 0:T], start=(j == 0), stop=(j == 1))
                i.then_inc(var_ready, 1)

                def turn_rows(t, turned_to):
                    for c, (a, n) in enumerate(((0, P), (P, P), (TP, TS))):
                        for j in range(2):
                            i = turn(ps[0:n, 4 + c // 2, (c % 2) * 256 + j * P:(c % 2) * 256 + (j + 1) * P],
                                     proj[:, t + j, a:a + n])
                    i.then_inc(turned_to, 1)

                mod_step(l, 1, MOD_BLOCKS)
                pe.wait_ge(vb_ready, upto(l, vb_ready))
                pe.wait_ge(swap_read, upto(l, swap_read))
                turn_rows(BV, vb_turned)
                pe.wait_ge(vb_tok, upto(l, vb_tok))
                pe.wait_ge(spatial_masked, upto(l, spatial_masked))
                for g in range(4):
                    r = 64 * (g % 2)
                    for c, (a, n) in enumerate(((0, P), (P, P), (TP, TS))):
                        i = mm(ps[r:r + 64, 6 + g // 2, a:a + n], vt[0:n, c, g * 64:(g + 1) * 64], wsp[0:n, g, 0:n],
                               start=True, stop=True, skip_group_check=True)
                i.then_inc(spatial_ready, 1)

                turn_rows(DV, v_turned)
                pe.wait_ge(kv_d_loaded, upto(l, kv_d_loaded))
                pe.wait_ge(b_summed, upto(l, b_summed))
                pe.sem_inc(settled, 1)
                for h in range(NH):
                    j, r = h // 2, 64 * (h % 2)
                    i = mm(ps[0:TS, 6 + h % 2, j * TS:(j + 1) * TS], proj[r:r + 64, DK + j, TP:T], proj[r:r + 64, DQ + j, TP:T],
                           start=(j == 0), stop=True, skip_group_check=True)
                i.then_inc(znew_ready, 1)

                def d_scores(h):
                    j, r, z = h // 2, 64 * (h % 2), 2 + h % 2
                    if h >= 2:
                        pe.wait_ge(wt_ready, upto(l, wt_ready, h - 1))
                    k, q = proj[r:r + 64, DK + j, :], proj[r:r + 64, DQ + j, :]
                    mm(ps[:, z, 0:TP], k[:, 0:P], q[:, 0:TP], start=True, stop=True, skip_group_check=True)
                    mm(ps[:, z, TP:3 * P], k[:, P:TP], q[:, P:TP], start=False, stop=True, skip_group_check=True)
                    for b in range(4):
                        i = mm(ps[:, z, 3 * P + b * TS:3 * P + (b + 1) * TS], kv0k[r:r + 64, j, b * P:(b + 1) * P],
                               q[:, TP:T], start=False, stop=True, skip_group_check=True)
                    i.then_inc(z_ready, 1)

                def d_log_weights(h):
                    z, b = 2 + h % 2, h % 2
                    pe.wait_ge(keep_ready, upto(l, keep_ready, h + 1))
                    ntri, nones = cst[:, C_NTRI:C_NTRI + P], cst[:, C_NONE:C_NONE + P]
                    kw = dict(start=False, stop=True, skip_group_check=True)
                    mm(ps[:, z, :], ntri, d_keep[:, b, :], **kw)
                    mm(ps[:, z, P:TP], nones, d_keep[:, b, TP:3 * P], **kw)
                    for c in range(1, 4):
                        src = d_keep[:, b, 3 * P + c * TS:3 * P + (c + 1) * TS].unsqueeze(1).broadcast_to([P, c, TS])
                        mm(ps[:, z, 3 * P:3 * P + c * TS].rearrange("p (c n) -> p c n", c=c), nones, src, **kw)
                    new = d_new[:, 0, new_at(h):new_at(h) + TS].unsqueeze(1).broadcast_to([TS, 4, TS])
                    mm(ps[:, z, 3 * P:4 * P].rearrange("p (c n) -> p c n", c=4), nones[0:TS, :], new, **kw).then_inc(logw_ready, 1)

                def d_values(h):
                    j, r, b = h // 2, 64 * (h % 2), h % 2
                    bank = 6 if j == 0 else 5
                    pe.wait_ge(wt_ready, upto(l, wt_ready, h + 1))
                    c = slice(h * 64, (h + 1) * 64)
                    kw = dict(skip_group_check=True)
                    mm(ps[r:r + 64, bank, 0:TP], vt[:, 0, c], d_wt[:, b, 0:TP], start=True, stop=False, **kw)
                    mm(ps[r:r + 64, bank, P:TP], vt[:, 1, c], d_wt[:, b, TP:3 * P], start=False, stop=True, **kw)
                    for k in range(4):
                        mm(ps[r:r + 64, bank, TP:T], kv0v[:, k, c], d_wt[:, b, 3 * P + k * TS:3 * P + (k + 1) * TS],
                           start=False, stop=False, **kw)
                    mm(ps[r:r + 64, bank, TP:T], vt[0:TS, 2, c], d_new[:, 1, new_at(h):new_at(h) + TS],
                             start=False, stop=True, **kw).then_inc(d_out, 1)

                d_scores(0)
                mod_step(l, 2, MOD_BLOCKS)
                pe.wait_ge(znew_keep, upto(l, znew_keep))
                pe.sem_inc(settled, 1)
                for b in range(2):
                    i = mm(ps[0:TS, 6 + b, 0:2 * TS], cst[0:TS, C_NTRI:C_NTRI + TS], d_new[:, 0, b * 64:(b + 1) * 64],
                           start=False, stop=True, skip_group_check=True)
                i.then_inc(znew_logw, 1)
                d_scores(1)
                pe.wait_ge(v_tok, upto(l, v_tok, 1))
                pe.wait_ge(wnew_ready, upto(l, wnew_ready))
                for h in range(NH):
                    d_log_weights(h)
                    d_values(h)
                    if h + 2 < NH:
                        d_scores(h + 2)

                def attention(n, k_t, kc, vc, forget):
                    for c in range(3):
                        u = 3 * n + c
                        nk, blocks = ((P, 1), (2 * P, 2), (PAST + TS, 5))[c]
                        if c == 0:
                            pe.wait_ge(v_tok, upto(l, v_tok, 2 + n))
                        if u:
                            pe.wait_ge(exp_ready, upto(l, exp_ready, u))
                        pe.wait_ge(queries_ready, upto(l, queries_ready, n + 1))
                        if n:
                            pe.wait_ge(chosen, upto(l, chosen, c + 1))
                        pe.sem_inc(settled, 1)
                        if c < 2:
                            per = 512 // nk
                            for h in range(NH):
                                o = flat[:, 1024 + h * nk:1024 + (h + 1) * nk]
                                i = mm(o, queries[:, h, c * P:(c + 1) * P], proj[:, k_t + h // 2, 0:nk],
                                       start=(h % per == 0), stop=(not forget), skip_group_check=True)
                                if forget:
                                    i = mm(o, fl8[:, h, c * P:(c + 1) * P], fr8[:, 0:nk], start=False, stop=True,
                                           skip_group_check=True)
                        else:
                            if not forget:
                                pe.wait_ge(kv_a_loaded, upto(l, kv_a_loaded))
                                rep = cst[0:TS, C_REP:C_REP + P]
                                mm(ps[:, 2, :], rep, score[0:TS, 3 * P:3 * P + PAST], start=True, stop=False, skip_group_check=True)
                                mm(ps[:, 3, 0:TS], rep, score[0:TS, 3 * P + PAST:3 * P + PAST + TS], start=True, stop=False,
                                   skip_group_check=True)
                            for h in range(NH):
                                j, o = h // 2, TS * h
                                q = queries[:, h, TP:T]
                                kw = dict(skip_group_check=True)
                                i = mm(ps[o:o + TS, 2, :], q, kc[:, j, :], start=forget, stop=(not forget), **kw)
                                i = mm(ps[o:o + TS, 3, 0:TS], q, proj[:, k_t + j, TP:T], start=forget,
                                       stop=(not forget), **kw)
                                if forget:
                                    mm(ps[o:o + TS, 2, :], fl8[:, h, TP:T], fr8[:, TP:TP + PAST], start=False, stop=True, **kw)
                                    i = mm(ps[o:o + TS, 3, 0:TS], fl8[:, h, TP:T], fr8[:, TP + PAST:], start=False,
                                           stop=True, **kw)
                        i.then_inc(logits, 1)
                        if u in (1, 2):
                            mod_step(l, 2 + u, MOD_BLOCKS)
                        pe.wait_ge(probs_ready, upto(l, probs_ready, u + 1))
                        if c < 2:
                            for h in range(NH):
                                for b in range(blocks):
                                    g = h * blocks + b
                                    i = turn(ps[:, 4 + g // 4, (g % 4) * P:(g % 4 + 1) * P],
                                             probs[:, g * P:(g + 1) * P])
                        else:
                            for b in range(4):
                                turn(ps[:, 4, b * P:(b + 1) * P], probs[:, b * P:(b + 1) * P])
                            i = turn(ps[0:TS, 5, 0:P], probs[:, PAST:PAST + TS])
                        i.then_inc(turned, 1)
                        pe.wait_ge(probs_tok, upto(l, probs_tok, u + 1))
                        if c == 0:
                            pe.wait_ge(ol_ready, upto(l, ol_ready, 4 + 2 * n))
                        for h in range(NH):
                            j, r = h // 2, 64 * (h % 2)
                            v = slice(h * 64, (h + 1) * 64)
                            if c < 2:
                                for b in range(blocks):
                                    i = mm(ps[r:r + 64, 6 + j, c * P:(c + 1) * P], vt[:, b, v],
                                           probs_t[:, h * blocks + b, :], start=(b == 0), stop=(b == blocks - 1),
                                           skip_group_check=True)
                            else:
                                q = slice(h * TS, (h + 1) * TS)
                                for b in range(4):
                                    mm(ps[r:r + 64, 6 + j, TP:T], vc[:, b, v], probs_t[:, b, q], start=(b == 0),
                                       stop=False, skip_group_check=True)
                                i = mm(ps[r:r + 64, 6 + j, TP:T], vt[0:TS, 2, v], probs_t[0:TS, 4, q], start=False,
                                       stop=True, skip_group_check=True)
                        i.then_inc(pv_done, 1)

                pe.wait_ge(ol_ready, upto(l, ol_ready, 4))
                turn_rows(CV, v_turned)
                pe.wait_ge(f_ready, upto(l, f_ready))
                pe.wait_ge(kv_c_loaded, upto(l, kv_c_loaded))
                attention(0, CK, kv1k, kv1v, True)

                pe.wait_ge(roped, upto(l, roped))
                pe.wait_ge(exp_ready, upto(l, exp_ready, 3))
                pe.wait_ge(probs_tok, upto(l, probs_tok, 3))
                for c in range(3):
                    for h in range(IH):
                        n = c * IH + h
                        if n >= 2:
                            pe.wait_ge(relued, upto(l, relued, n - 1))
                            pe.sem_inc(settled, 1)
                        j, r, b = h // 4, 32 * (h % 4), 2 + 2 * (h % 2)
                        if c < 2:
                            i = mm(ps[:, b, 0:(c + 1) * P], proj[r:r + 32, AQI + j, c * P:(c + 1) * P],
                                   proj[r:r + 32, AKI, 0:(c + 1) * P], start=True, stop=True)
                        else:
                            q = proj[r:r + 32, AQI + j, TP:T]
                            mm(ps[0:TS, b, :], q, kix[r:r + 32, :], start=True, stop=True)
                            i = mm(ps[0:TS, b + 1, 0:TS], q, proj[r:r + 32, AKI, TP:T], start=True, stop=True)
                        i.then_inc(dots, 1)
                mod_step(l, 5, MOD_BLOCKS)
                pe.wait_ge(relued, upto(l, relued))
                turn_rows(AV, v_turned)
                for j in range(6, MOD_BLOCKS + 1):
                    mod_step(l, j, MOD_BLOCKS)
                attention(1, AK, kv0k, kv0v, False)

                pe.wait_ge(mod_ready, upto(l, mod_ready))
                pe.sem_inc(settled, 1)
                tiles(Q_GATE, 4 * KT, NIN)

                pe.wait_ge(ol_ready, upto(l, ol_ready))
                for p in range(8):
                    q, b = Q_BRANCH + p, p // 2
                    pe.wait_ge(lo_ready, upto(l, lo_ready, q + 1))
                    for m in range(4):
                        t = NIN + 4 * KT + 4 * p + m
                        pe.wait_ge(bank_free[t % 2], taken(l, t // 2))
                        terms = [(k, oh[:, 2 * b + k, :], ol[:, 2 * b + k, :]) for k in range(2)]
                        product(ps[:, t % 2, 0:T], q % RING, (4, m, True, True), terms).then_inc(piece_done, 1)

                pe.wait_ge(merged_l, upto(l, merged_l))
                pe.sem_inc(settled, 1)
                tiles(Q_OUT, KT, NIN + 8 * KT)

                sums(2)
                pe.wait_ge(hl_ready, upto(l, hl_ready, 2))


                def up_piece(slot, q, bank, copied):
                    pe.wait_ge(lo_ready, upto(l, lo_ready, q + 1))
                    if copied is None:
                        pe.wait_ge(bank_free[bank], taken(l, (NIN + 9 * KT) // 2))
                    else:
                        pe.wait_ge(up_copied, upto(l, up_copied, copied))
                    product(ps[:, bank, 0:T], slot, (1, 0, True, True), h_terms).then_inc(piece_done, 1)

                for j in range(RING):
                    up_piece((Q_UP + j) % RING, Q_UP + j, j % 2, None if j < 2 else j - 1)
                with pe.Fori(0, 2 * FT // RING - 1) as r:
                    for j in range(RING):
                        up_piece((Q_UP + j) % RING, r * RING + (Q_UP + RING + j), j % 2, r * RING + (RING + j - 1))
                pe.wait_ge(up_copied, upto(l, up_copied))
                pe.wait_ge(fal_ready, upto(l, fal_ready))
                pe.sem_inc(settled, 1)
                with pe.Fori(0, 2) as r:
                    for m in range(4):
                        k0 = 0
                        t = NIN + 9 * KT + m
                        pe.wait_ge(bank_free[t % 2], taken(l, r * 2 + t // 2))
                        for c in range(3):
                            n = 3 * m + c
                            pe.wait_ge(lo_ready, upto(l, lo_ready, r * 12 + Q_DOWN + n + 1))
                            terms = [(k, fah[:, k0 + k, :], fal[:, k0 + k, :]) for k in range(DOWN_SPLIT[c])]
                            product(ps[:, t % 2, 0:CC], (Q_DOWN + n) % RING, (1, 0, c == 0, c == 2), terms).then_inc(piece_done, 1)
                            k0 += DOWN_SPLIT[c]

            pe.wait_ge(fin[0], 1)
            for k in range(KT):
                i = mm(ps[:, 7, 0:T], cst[:, C_ONE:C_ONE + P], work[:, k, :], start=(k == 0), stop=(k == KT - 1))
            i.then_inc(fin[1], 1)

        @block.scalar
        def _(act):
            A = nc.scalar.activation
            eps = cst[:, C_EPS:C_EPS + 1]
            act.wait_ge(start_loaded, 80)
            A(cmod[:, :, 2:4], cmod[:, :, 0:2], ACT.Exp, scale=-1.0).then_inc(c_exp, 1)
            with act.Fori(0, DEPTH) as l:
                count = [0]

                def in_order(ins, at=0):
                    count[0] += 1
                    ins.then_inc(act_own, 1)
                    act.wait_ge(act_own, l * ACT_LINKS + (count[0] + at))

                def high(q, slot, first=False):
                    act.wait_ge(raw_loaded[slot], loaded(l, slot, place_of(q)))
                    if first:
                        act.wait_ge(piece_done, upto(l, piece_done, 0))
                    else:
                        act.wait_ge(piece_done, upto(l, piece_done, done(q - RING, 3)))
                    A(whi[:, slot, :], raw[:, slot, :], ACT.Copy).then_inc(hi_ready, 1)

                def high_in_loop(r, q, k, step):
                    slot = q % RING
                    act.wait_ge(raw_loaded[slot], loaded(l, slot, place_of(q), r * (16 * step // RING)))
                    act.wait_ge(piece_done, upto(l, piece_done, r * step + k))
                    A(whi[:, slot, :], raw[:, slot, :], ACT.Copy).then_inc(hi_ready, 1)

                def split_pieces(a, b):
                    for q in range(a, b):
                        if q + AHEAD < NSPLIT:
                            high(q + AHEAD, (q + AHEAD) % RING, q + AHEAD < RING)

                def split_loop(a, b):
                    n = (b - a) // RING
                    with act.Fori(0, n) as r:
                        for j in range(RING):
                            q = a + j + AHEAD
                            high_in_loop(r, q, done(q - RING, 3), RING)
                    split_pieces(a + n * RING, b)

                def norm(n):
                    act.wait_ge(bank_free[0], taken(l, (0 if n == 1 else NIN + 9 * KT) // 2))
                    act.wait_ge(bank_free[1], taken(l, (0 if n == 1 else NIN + 9 * KT) // 2))
                    A(work[:], x[:], ACT.Square).then_inc(squared, 1)
                    act.wait_ge(sums_ready, upto(l, sums_ready, n))
                    in_order(A(rstd[:, 0, :], ps[:, 7, 0:T], ACT.Ln, scale=1.0 / DM, bias=eps))
                    A(rstd[:, 0, :], rstd[:, 0, :], ACT.Exp, scale=-0.5).then_inc(rstd_guess, 1)
                    act.wait_ge(h_scaled, upto(l, h_scaled, n))
                    A(hh[:], work[:], ACT.Copy).then_inc(hh_ready, 1)

                for q in range(AHEAD):
                    high(q, q, True)
                norm(1)
                high(AHEAD, AHEAD, True)
                split_loop(1, NIN - AHEAD)

                act.wait_ge(bank_free[0], taken(l, (NIN) // 2))
                act.wait_ge(bank_free[1], taken(l, (NIN) // 2))
                A(proj[:, BU:BU + 4, :], proj[:, BU:BU + 4, :], ACT.Gelu_apprx_tanh).then_inc(gelued, 1)
                act.wait_ge(centred, upto(l, centred))
                A(scr[:, :, 0:T], proj[:, BV:BV + 2, :], ACT.Square).then_inc(centred_squared, 1)
                act.wait_ge(var_ready, upto(l, var_ready))
                in_order(A(rstd[:, 0, :], ps[:, 7, 0:T], ACT.Ln, scale=1.0 / 256, bias=eps))
                A(rstd[:, 0, :], rstd[:, 0, :], ACT.Exp, scale=-0.5).then_inc(b_guess, 1)

                def rows_out(taken_out):
                    A(vt[:, 0:2, :], ps[:, 4, :].rearrange("p (c n) -> p c n", c=2), ACT.Copy)
                    A(vt[0:TS, 2, :], ps[0:TS, 5, 0:256], ACT.Copy).then_inc(taken_out, 1)

                act.wait_ge(vb_turned, upto(l, vb_turned))
                rows_out(vb_tok)
                for j in range(2):
                    act.wait_ge(b_summed, upto(l, b_summed, j + 1))
                    A(oh[:, 2 + j, :], scr[:, j, 0:T], ACT.Copy).then_inc(oh_ready, 1)

                fx = fl8[:, 0, :]
                act.wait_ge(vecs_loaded, upto(l, vecs_loaded))
                in_order(A(fx, proj[FROW:FROW + 8, MISC, :], ACT.Abs, bias=vec[0:8, V_FB:V_FB + 1]))
                in_order(A(fx, fx, ACT.Exp, scale=-1.0))
                A(fx, fx, ACT.Ln, bias=1.0).then_inc(f_log, 1)

                act.wait_ge(v_turned, upto(l, v_turned, 1))
                act.wait_ge(spatial_ready, upto(l, spatial_ready))
                rows_out(v_tok)

                def soft_log(out, in_, logged):
                    in_order(A(out, in_, ACT.Abs))
                    in_order(A(out, out, ACT.Exp, scale=-1.0))
                    A(out, out, ACT.Ln, bias=1.0).then_inc(logged, 1)

                act.wait_ge(znew_ready, upto(l, znew_ready))
                soft_log(d_new[:, 0, :].rearrange("p (b n) -> p b n", b=2), znew, znew_log)
                for h in range(NH):
                    if h == 0:
                        act.wait_ge(z_ready, upto(l, z_ready, 1))
                        soft_log(d_keep[:, 0, :], ps[:, 2, :], z_log)
                        act.wait_ge(znew_logw, upto(l, znew_logw))
                        A(d_new[:, 1, :].rearrange("p (b n) -> p b n", b=2), znew, ACT.Exp).then_inc(wnew_ready, 1)
                    if h + 1 < NH:
                        act.wait_ge(z_ready, upto(l, z_ready, h + 2))
                        soft_log(d_keep[:, (h + 1) % 2, :], ps[:, 2 + (h + 1) % 2, :], z_log)
                    act.wait_ge(logw_ready, upto(l, logw_ready, h + 1))
                    if h >= 2:
                        act.wait_ge(d_out, upto(l, d_out, h - 1))
                    A(d_wt[:, h % 2, :], ps[:, 2 + h % 2, :], ACT.Exp).then_inc(wt_ready, 1)
                for j in range(2):
                    act.wait_ge(d_out, upto(l, d_out, 2 * j + 2))
                    A(oh[:, 6 + j, :], ps[:, 6 - j, 0:T], ACT.Copy).then_inc(oh_ready, 1)

                def softmaxes(n):
                    for c in range(3):
                        u = 3 * n + c
                        act.wait_ge(max_ready, upto(l, max_ready, u + 1))
                        if u:
                            act.wait_ge(turned, upto(l, turned, u))
                        if c < 2:
                            nk = (c + 1) * P
                            for h in range(NH):
                                i = A(probs[:, h * nk:(h + 1) * nk], flat[:, 1024 + h * nk:1024 + (h + 1) * nk], ACT.Exp,
                                      bias=small[:, h:h + 1], accum_out=small[:, 8 + h:9 + h])
                        else:
                            i = A(probs[:, 0:PAST + TS], flat[:, 1024:1024 + PAST + TS], ACT.Exp,
                                  bias=small[:, 0:1], accum_out=small[:, 8:9])
                        i.then_inc(exp_ready, 1)
                        act.wait_ge(turned, upto(l, turned, u + 1))
                        if u:
                            act.wait_ge(pv_done, upto(l, pv_done, u))
                        if c == 0:
                            i = A(probs_t[:, 0:4, :], ps[:, 4, :].rearrange("p (c n) -> p c n", c=4), ACT.Copy)
                        elif c == 1:
                            i = A(probs_t[:], ps[:, 4:6, :].rearrange("p b (c n) -> p (b c) n", c=4), ACT.Copy)
                        else:
                            A(probs_t[:, 0:4, :], ps[:, 4, :].rearrange("p (c n) -> p c n", c=4), ACT.Copy)
                            i = A(probs_t[0:TS, 4, :], ps[0:TS, 5, 0:P], ACT.Copy)
                        i.then_inc(probs_tok, 1)
                    if n == 1:
                        split_pieces(NIN - AHEAD, NIN)
                    act.wait_ge(pv_done, upto(l, pv_done, 3 * n + 3))
                    for j in range(2):
                        A(oh[:, 4 * (1 - n) + j, :], ps[:, 6 + j, 0:T], ACT.Copy).then_inc(oh_ready, 1)

                act.wait_ge(v_turned, upto(l, v_turned, 2))
                act.wait_ge(d_out, upto(l, d_out))
                rows_out(v_tok)
                softmaxes(0)

                for c in range(3):
                    for h in range(IH):
                        n = c * IH + h
                        act.wait_ge(dots, upto(l, dots, n + 1))
                        if n >= 2:
                            act.wait_ge(scored, upto(l, scored, n - 1))
                        b = 1024 * (1 + h % 2)
                        if c < 2:
                            i = A(scr[:, h % 2, 0:(c + 1) * P], flat[:, b:b + (c + 1) * P], ACT.Relu)
                        else:
                            i = A(scr[0:TS, h % 2, 0:PAST + TS], flat[0:TS, b:b + PAST + TS], ACT.Relu)
                        i.then_inc(relued, 1)
                act.wait_ge(v_turned, upto(l, v_turned, 3))
                act.wait_ge(pv_done, upto(l, pv_done, 3))
                rows_out(v_tok)
                softmaxes(1)

                split_loop(Q_GATE, Q_BRANCH)
                for b in range(4):
                    act.wait_ge(bank_free[0], taken(l, (NIN + (b + 1) * KT) // 2))
                    act.wait_ge(bank_free[1], taken(l, (NIN + (b + 1) * KT) // 2))
                    A(gates[:, b * KT:(b + 1) * KT, :], gates[:, b * KT:(b + 1) * KT, :], ACT.Sigmoid).then_inc(sigmoid_ready, 1)
                split_pieces(Q_BRANCH, Q_OUT)
                act.wait_ge(merged, upto(l, merged))
                A(hh[:], work[:], ACT.Copy).then_inc(merged_h, 1)
                split_pieces(Q_OUT, Q_UP)
                norm(2)

                def up_pair(p, odd, r=None):
                    for g in range(2):
                        u = 2 * odd + g
                        if r is None:
                            q = Q_UP + 2 * p + g + AHEAD
                            if q < NSPLIT:
                                high(q, q % RING)
                        else:
                            q = Q_UP + 2 * odd + 4 + g + AHEAD
                            high_in_loop(r, q, done(q - RING), RING)
                        act.wait_ge(piece_done, upto(l, piece_done, p * 2 + (done(Q_UP) + g)))
                        if r is not None or p >= 2:
                            act.wait_ge(convolved, upto(l, convolved, p * 2 + (g - 3)))
                        elif p == 0 and g == 0:
                            act.wait_ge(ol_ready, upto(l, ol_ready))
                        A(up[:, u, 2:2 + TP], ps[:, g, 0:TP], ACT.Copy)
                        A(up[:, u, 4 + TP:4 + T], ps[:, g, TP:T], ACT.Copy).then_inc(up_copied, 1)

                def silu(p, odd):
                    act.wait_ge(convolved, upto(l, convolved, p * 2 + 2))
                    A(sil[:, odd, :], conv[:, 2 * odd, :], ACT.Silu).then_inc(silued, 1)

                def product_high(p, odd):
                    act.wait_ge(product_ready, upto(l, product_ready, p + 1))
                    A(fah[:, bass.ds(p, 1), :] if not isinstance(p, int) else fah[:, p:p + 1, :],
                            prod[:, odd:odd + 1, :], ACT.Copy).then_inc(fah_ready, 1)

                act.wait_ge(proj_stored, upto(l, proj_stored))
                up_pair(0, 0)
                up_pair(1, 1)
                silu(0, 0)
                with act.Fori(0, FT // 2 - 1) as r:
                    for odd in range(2):
                        p = r * 2 + (2 + odd)
                        up_pair(p, odd, r)
                        product_high(r * 2 + odd, odd)
                        silu(r * 2 + (1 + odd), 1 - odd)
                product_high(FT - 2, 0)
                silu(FT - 1, 1)
                product_high(FT - 1, 1)
                split_pieces(Q_DOWN, Q_DOWN + 1)
                split_loop(Q_DOWN + 1, NSPLIT - AHEAD)
                assert count[0] == ACT_LINKS, ("ACT_LINKS", count[0])

            for b in range(2):
                act.wait_ge(bank_free[b], DEPTH * TILES2 + 1)
            A(work[:], x[:], ACT.Square).then_inc(fin[0], 1)
            act.wait_ge(fin[1], 1)
            A(rstd[:, 0, :], ps[:, 7, 0:T], ACT.Ln, scale=1.0 / DM, bias=eps).then_inc(fin[2], 1)
            act.wait_ge(fin[2], 1)
            A(rstd[:, 0, :], rstd[:, 0, :], ACT.Exp, scale=-0.5).then_inc(fin[3], 1)

        @block.vector
        def _(dve):
            V = nc.vector
            dve.wait_ge(start_loaded, 80)
            dve.wait_ge(c_exp, 1)
            cs = cmod[:, :, 2:4]
            V.tensor_scalar(cs, cs, 1.0, None, ALU.add).then_inc(c_ready, 1)
            dve.wait_ge(c_ready, 1)
            V.reciprocal(cs, cs).then_inc(c_ready, 1)
            dve.wait_ge(c_ready, 2)
            V.tensor_tensor(cs, cs, cmod[:, :, 0:2], ALU.mult).then_inc(c_sig, 1)

            def newton(link, scale):
                y, v = rstd[:, 0, :], rstd[:, 1, :]
                link(V.tensor_scalar(v, ps[:, 7, 0:T], scale, EPS, ALU.mult, ALU.add))
                link(V.tensor_tensor(v, v, y, ALU.mult))
                link(V.tensor_tensor(v, v, y, ALU.mult))
                link(V.tensor_scalar(v, v, -0.5, 1.5, ALU.mult, ALU.add))
                link(V.tensor_tensor(y, y, v, ALU.mult))

            def mod_take(l, j):
                dve.wait_ge(mod_read, 4 * j + 4 if l is None else upto(l, mod_read, 4 * j + 4))
                V.tensor_copy(mod_rows[j % 2], ps[32:34, j % 2, :]).then_inc(rows_taken, 1)

            def mod_add(l, j):
                dve.wait_ge(rows_turned, j + 1 if l is None else upto(l, rows_turned, j + 1))
                if l is None:
                    m, at = 4 * j, slice(4 * j, 4 * j + 4)
                else:
                    m = (MOD_A + 4 * j) % NMOD
                    at = bass.ds(l * NMV + (m if m >= MOD_A else NMV + m), 4)
                V.tensor_tensor(mod[:, m:m + 4, :], ps[:, j % 2, 0:8].rearrange("p (m g) -> p m g", g=2),
                                mvec[:, at].unsqueeze(2).broadcast_to([P, 4, 2]), ALU.add).then_inc(mod_ready, 1)

            def mod_step(l, j, blocks):
                if 2 <= j < blocks + 2:
                    mod_add(l, j - 2)
                if 1 <= j < blocks + 1:
                    mod_take(l, j - 1)

            def norm_scale(link, n, scale_at, g_at):
                link(V.tensor_scalar(norm_a[:, n], mod[:, scale_at:scale_at + KT, :], 1.0, None, ALU.add))
                link(V.tensor_tensor(norm_a[:, n], norm_a[:, n], mvec[:, g_at].unsqueeze(2).broadcast_to([P, KT, 2]), ALU.mult))

            for j in range(FIRST_BLOCKS + 2):
                mod_step(None, j, FIRST_BLOCKS)
            dve.wait_ge(mod_ready, FIRST_BLOCKS)
            links = [2]

            def first_link(ins):
                links[0] += 1
                ins.then_inc(c_ready, 1)
                dve.wait_ge(c_ready, links[0])

            norm_scale(first_link, 0, KT, slice(M_G1, M_G1 + KT))

            with dve.Fori(0, DEPTH) as l:
                count = [0]

                def in_order(ins, at=0):
                    count[0] += 1
                    ins.then_inc(dve_own, 1)
                    dve.wait_ge(dve_own, l * DVE_LINKS + (count[0] + at))

                dve.wait_ge(vecs_loaded, upto(l, vecs_loaded))
                V.tensor_tensor(wsp[:], wsp[:], cst[:, C_SPAT:C_SPAT + P].unsqueeze(1).broadcast_to([P, 4, P]), ALU.mult).then_inc(spatial_masked, 1)

                def norm(n):
                    shift_at = 0 if n == 1 else 24
                    dve.wait_ge(rstd_guess, upto(l, rstd_guess, n))
                    newton(in_order, 1.0 / DM)
                    in_order(V.tensor_tensor(work[:], x[:], rstd[:, 0:1, :].broadcast_to([P, KT, T]), ALU.mult))
                    for k in range(KT):
                        for g, (a, b) in enumerate(((0, TP), (TP, T))):
                            i = V.tensor_scalar(work[:, k, a:b], work[:, k, a:b], norm_a[:, n - 1, k, g:g + 1],
                                                mod[:, shift_at + k, g:g + 1], ALU.mult, ALU.add)
                    i.then_inc(h_scaled, 1)
                    dve.wait_ge(hh_ready, upto(l, hh_ready, n))
                    V.tensor_tensor(hl[:], work[:], hh[:].bitcast(F32), ALU.subtract).then_inc(hl_ready, 1)

                norm(1)

                def take_proj(t, bank):
                    dve.wait_ge(piece_done, upto(l, piece_done, t + 1))
                    i = V.tensor_scalar(proj[:, bass.ds(t, 1), :], ps[:, bank:bank + 1, 0:T],
                                        cst[:, bass.ds(t + C_QS, 1)], None, ALU.mult)
                    return i

                with dve.Fori(0, NIN // 2) as r:
                    for b in range(2):
                        take_proj(r * 2 + b, b).then_inc(bank_free[b], 1)
                dve.wait_ge(bank_free[0], taken(l, (NIN) // 2))
                dve.wait_ge(bank_free[1], taken(l, (NIN) // 2))

                for n, t in enumerate((AQ, AQ + 1, AK, AK + 1, AQI, AQI + 1, AKI)):
                    cos, sin = (C_COSA, C_SINA) if n < 4 else (C_COSI, C_SINI)
                    dve.wait_ge(swapped, upto(l, swapped, n + 1))
                    if n >= 2:
                        dve.wait_ge(roped, upto(l, roped, n - 1))
                    V.tensor_tensor(scr[:, n % 2, 0:T], ps[:, 4 + n % 2, 0:T], cst[:, sin:sin + T], ALU.mult).then_inc(swap_read, 1)
                    dve.wait_ge(swap_read, upto(l, swap_read, n + 1))
                    in_order(V.tensor_tensor(proj[:, t, :], proj[:, t, :], cst[:, cos:cos + T], ALU.mult))
                    V.tensor_tensor(proj[:, t, :], proj[:, t, :], scr[:, n % 2, 0:T], ALU.add).then_inc(roped, 1)
                dve.wait_ge(w_turned, upto(l, w_turned))
                V.tensor_copy(small[:, 16:32], ps[:, 7, 0:16])
                V.tensor_copy(small[0:TS, 32:40], ps[0:TS, 7, 16:24]).then_inc(w_read, 1)

                mod_step(l, 0, MOD_BLOCKS)
                dve.wait_ge(mean_ready, upto(l, mean_ready))
                for j in range(2):
                    i = V.scalar_tensor_tensor(proj[:, BV + j, :], ps[:, 7, 0:T], -1.0 / 256, proj[:, BV + j, :], ALU.mult, ALU.add)
                i.then_inc(centred, 1)
                mod_step(l, 1, MOD_BLOCKS)
                dve.wait_ge(b_guess, upto(l, b_guess))
                newton(in_order, 1.0 / 256)
                in_order(V.tensor_tensor(proj[:, BV:BV + 2, :], proj[:, BV:BV + 2, :],
                                       rstd[:, 0:1, :].broadcast_to([P, 2, T]), ALU.mult))
                for j in range(2):
                    i = V.tensor_scalar(proj[:, BV + j, :], proj[:, BV + j, :], vec[:, V_LG + j:V_LG + j + 1],
                                        vec[:, V_LB + j:V_LB + j + 1], ALU.mult, ALU.add)
                i.then_inc(vb_ready, 1)
                dve.wait_ge(spatial_ready, upto(l, spatial_ready))
                for j in range(2):
                    bs = vec[:, V_BS + j * P:V_BS + (j + 1) * P]
                    V.tensor_tensor(scr[:, j, 0:TP].rearrange("p (c n) -> p c n", c=2),
                                    ps[:, 6 + j, 0:TP].rearrange("p (c n) -> p c n", c=2),
                                    bs.unsqueeze(1).broadcast_to([P, 2, P]), ALU.add)
                    in_order(V.tensor_tensor(scr[:, j, TP:T], ps[:, 6 + j, TP:T], bs[:, 0:TS], ALU.add))
                    V.tensor_tensor(scr[:, j, 0:T], scr[:, j, 0:T], proj[:, BU + j, :], ALU.mult).then_inc(b_summed, 1)
                for j in range(2):
                    dve.wait_ge(oh_ready, upto(l, oh_ready, j + 1))
                    V.tensor_tensor(ol[:, 2 + j, :], scr[:, j, 0:T], oh[:, 2 + j, :].bitcast(F32), ALU.subtract).then_inc(ol_ready, 1)

                in_order(V.tensor_scalar(lf[:], proj[FROW:FROW + 8, MISC, :], vec[0:8, V_FB:V_FB + 1], 0.0, ALU.add, ALU.min))
                dve.wait_ge(f_log, upto(l, f_log))
                ones8 = lambda n: cst[0:8, C_ONE:C_ONE + 1].broadcast_to([8, n])
                in_order(V.tensor_tensor(lf[:], lf[:], fl8[:, 0, :], ALU.subtract))
                in_order(V.tensor_tensor_scan(fcum[:, 0:TP], ones8(TP), lf[:, 0:TP], 0.0, ALU.mult, ALU.add))
                in_order(V.tensor_tensor_scan(fcum[:, TP:TP + PAST], ones8(PAST), lfp[:], 0.0, ALU.mult, ALU.add))
                in_order(V.tensor_tensor_scan(fcum[:, TP + PAST:], ones8(TS), lf[:, TP:T],
                                            fcum[:, TP + PAST - 1:TP + PAST], ALU.mult, ALU.add))
                V.tensor_scalar(fr8[:], fcum[:], cst[0:8, C_FR:C_FR + 1], cst[0:8, C_FR + 1:C_FR + 2], ALU.mult, ALU.add)
                for h in range(NH):
                    a, b = (cst[0:8, C_FL + 2 * h + i:C_FL + 2 * h + i + 1] for i in range(2))
                    V.tensor_scalar(fl8[:, h, 0:TP], fcum[:, 0:TP], a, b, ALU.mult, ALU.add)
                    i = V.tensor_scalar(fl8[:, h, TP:T], fcum[:, TP + PAST:], a, b, ALU.mult, ALU.add)
                i.then_inc(f_ready, 1)

                strict, strict1 = cst[:, C_STRICT:C_STRICT + P], cst[:, C_STRICT1:C_STRICT1 + P]
                mod_step(l, 2, MOD_BLOCKS)
                dve.wait_ge(znew_log, upto(l, znew_log))
                keep = d_new[:, 0, :].rearrange("p (b n) -> p b n", b=2)
                in_order(V.scalar_tensor_tensor(keep, znew, 0.0, keep, ALU.max, ALU.add))
                n4 = lambda ap: ap.rearrange("p (h n) -> p h n", h=NH)
                z4 = znew.rearrange("p b (j n) -> p b j n", j=2)
                V.tensor_tensor(z4, z4, strict[0:TS, 0:TS].unsqueeze(1).unsqueeze(1).broadcast_to([TS, 2, 2, TS]), ALU.add)
                V.tensor_tensor(n4(d_new[:, 0, :]), n4(d_new[:, 0, :]),
                                      strict1[0:TS, 0:TS].unsqueeze(1).broadcast_to([TS, NH, TS]), ALU.mult).then_inc(znew_keep, 1)
                for h in range(NH):
                    b = h % 2
                    z = ps[:, 2 + b, :]
                    diag = lambda ap: ap.rearrange("p (a n) -> p a n", n=P)[:, 0:3:2, :]
                    dve.wait_ge(z_log, upto(l, z_log, h + 1))
                    in_order(V.scalar_tensor_tensor(d_keep[:, b, :], z, 0.0, d_keep[:, b, :], ALU.max, ALU.add))
                    V.tensor_tensor(diag(z), diag(z), strict.unsqueeze(1).broadcast_to([P, 2, P]), ALU.add)
                    V.tensor_tensor(diag(d_keep[:, b, :]), diag(d_keep[:, b, :]),
                                          strict1.unsqueeze(1).broadcast_to([P, 2, P]), ALU.mult).then_inc(keep_ready, 1)
                for j in range(2):
                    dve.wait_ge(oh_ready, upto(l, oh_ready, 3 + j))
                    V.tensor_tensor(ol[:, 6 + j, :], ps[:, 6 - j, 0:T], oh[:, 6 + j, :].bitcast(F32), ALU.subtract).then_inc(ol_ready, 1)

                def softmaxes(n, q_t):
                    for h in range(NH):
                        i = V.tensor_scalar(queries[:, h, :], proj[:, q_t + h // 2, :],
                                            cst[:, C_HALF + h % 2:C_HALF + h % 2 + 1], None, ALU.mult)
                    i.then_inc(queries_ready, 1)
                    for c in range(3):
                        u = 3 * n + c
                        nk = (P, 2 * P, PAST + TS)[c]
                        if u in (1, 2):
                            mod_step(l, 2 + u, MOD_BLOCKS)
                        dve.wait_ge(logits, upto(l, logits, u + 1))
                        if c < 2:
                            lg = flat[:, 1024:1024 + NH * nk].rearrange("p (h k) -> p h k", h=NH)
                            if n == 0:
                                d = lg[:, :, c * P:(c + 1) * P]
                                in_order(V.tensor_tensor(d, d, cst[:, C_CAUSAL:C_CAUSAL + P].unsqueeze(1).broadcast_to([P, NH, P]), ALU.add))
                            else:
                                m = score[:, c * P:c * P + nk]
                                in_order(V.tensor_tensor(lg, lg, m.unsqueeze(1).broadcast_to([P, NH, nk]), ALU.add))
                            V.tensor_reduce(small[:, 0:NH], lg, X, ALU.max, negate=True).then_inc(max_ready, 1)
                        else:
                            lg = flat[:, 1024:1024 + nk]
                            if n == 0:
                                in_order(V.tensor_tensor(lg[:, PAST:], lg[:, PAST:], cst[:, C_NEW:C_NEW + TS], ALU.add))
                            V.tensor_reduce(small[:, 0:1], lg, X, ALU.max, negate=True).then_inc(max_ready, 1)
                        dve.wait_ge(exp_ready, upto(l, exp_ready, u + 1))
                        if c < 2:
                            in_order(V.reciprocal(small[:, 12:12 + NH], small[:, 8:8 + NH]))
                            e = probs[:, 0:NH * nk].rearrange("p (h k) -> p h k", h=NH)
                            i = V.tensor_tensor(e, e, small[:, 12:12 + NH].unsqueeze(2).broadcast_to([P, NH, nk]), ALU.mult)
                        else:
                            in_order(V.reciprocal(small[:, 12:13], small[:, 8:9]))
                            i = V.tensor_scalar(probs[:, 0:nk], probs[:, 0:nk], small[:, 12:13], None, ALU.mult)
                        i.then_inc(probs_ready, 1)
                    for j in range(2):
                        dve.wait_ge(oh_ready, upto(l, oh_ready, 5 + 2 * n + j))
                        t = 4 * (1 - n) + j
                        V.tensor_tensor(ol[:, t, :], ps[:, 6 + j, 0:T], oh[:, t, :].bitcast(F32), ALU.subtract).then_inc(ol_ready, 1)

                softmaxes(0, CQ)

                parts = ((0, P, P), (P, 2 * P, P), (3 * P, PAST + TS, TS))
                for c, (a, nk, m) in enumerate(parts):
                    s = score[0:m, a:a + nk]
                    for h in range(IH):
                        n = c * IH + h
                        w = small[0:m, 16 + 8 * c + h:17 + 8 * c + h]
                        dve.wait_ge(relued, upto(l, relued, n + 1))
                        if h == 0:
                            i = V.tensor_scalar(s, scr[0:m, h % 2, 0:nk], w, None, ALU.mult)
                        else:
                            i = V.scalar_tensor_tensor(s, scr[0:m, h % 2, 0:nk], w, s, ALU.mult, ALU.add)
                        i.then_inc(scored, 1)
                        dve.wait_ge(scored, upto(l, scored, n + 1))
                    if c < 2:
                        d = score[:, a + c * P:a + (c + 1) * P]
                        in_order(V.tensor_tensor(d, d, cst[:, C_ADM:C_ADM + P], ALU.add))
                mod_step(l, 5, MOD_BLOCKS)
                step_at = (4, 8, 12, 16, 20, 23, 27, 30)
                done_rounds = 0
                for c, (a, nk, m) in enumerate(parts):
                    s = score[0:m, a:a + nk]
                    best = small[0:m, 40:48]
                    for _ in range(SEL_P if c < 2 else SEL_S):
                        if done_rounds in step_at:
                            mod_step(l, 6 + step_at.index(done_rounds), MOD_BLOCKS)
                        done_rounds += 1
                        dve.sem_inc(settled, 1)
                        in_order(V.max(best, s))
                        dve.sem_inc(settled, 1)
                        in_order(V.match_replace(s, best, s, TAKEN))
                    V.tensor_scalar(s, s, 0.5 * (TAKEN + INADMISSIBLE), MASKED, ALU.is_gt, ALU.mult).then_inc(chosen, 1)
                    dve.wait_ge(chosen, upto(l, chosen, c + 1))
                dve.wait_ge(mod_ready, upto(l, mod_ready))
                norm_scale(in_order, 0, KT, bass.ds(l * NMV + (NMV + M_G1), KT))
                norm_scale(in_order, 1, 4 * KT, bass.ds(l * NMV + M_G2, KT))
                softmaxes(1, AQ)

                with dve.Fori(0, 4 * KT // 2) as r:
                    for b in range(2):
                        dve.wait_ge(piece_done, upto(l, piece_done, r * 2 + (Q_GATE + b + 1)))
                        V.tensor_scalar(gates[:, bass.ds(r * 2 + b, 1), :], ps[:, b:b + 1, 0:T],
                                        vec[:, bass.ds(r * 2 + (V_GATE + b), 1)], None, ALU.add).then_inc(bank_free[b], 1)

                for t in range(4 * KT):
                    b, m, k = t // KT, t % KT, t % 2
                    dve.wait_ge(piece_done, upto(l, piece_done, Q_BRANCH + t + 1))
                    if m == 0:
                        dve.wait_ge(sigmoid_ready, upto(l, sigmoid_ready, b + 1))
                    if b == 0:
                        V.tensor_tensor(work[:, m, :], ps[:, k, 0:T], gates[:, t, :], ALU.mult).then_inc(bank_free[k], 1)
                    else:
                        V.tensor_tensor(gates[:, t, :], ps[:, k, 0:T], gates[:, t, :], ALU.mult).then_inc(bank_free[k], 1)
                        dve.wait_ge(bank_free[k], taken(l, (NIN + 4 * KT + t) // 2 + 1))
                        i = V.tensor_tensor(work[:, m, :], work[:, m, :], gates[:, t, :], ALU.add)
                        if t == 4 * KT - 1:
                            i.then_inc(merged, 1)
                dve.wait_ge(merged_h, upto(l, merged_h))
                V.tensor_tensor(hl[:], work[:], hh[:].bitcast(F32), ALU.subtract).then_inc(merged_l, 1)

                def add_out(m, bank, gate_at, cols, group_inc):
                    for g, ((a, b), c) in enumerate(zip(((0, TP), (TP, T)), cols)):
                        i = V.scalar_tensor_tensor(x[:, m, a:b], ps[:, bank, c:c + b - a], mod[:, gate_at + m, g:g + 1],
                                                   x[:, m, a:b], ALU.mult, ALU.add)
                    i.then_inc(bank_free[bank], 1)

                for m in range(KT):
                    dve.wait_ge(piece_done, upto(l, piece_done, done(Q_OUT + m)))
                    add_out(m, m % 2, 16, (0, TP), None)
                dve.wait_ge(bank_free[0], taken(l, (NIN + 9 * KT) // 2))
                dve.wait_ge(bank_free[1], taken(l, (NIN + 9 * KT) // 2))
                norm(2)

                dve.wait_ge(tail_stored, upto(l, tail_stored, 0))
                in_order(V.memset(up[:, :, 0:2], 0.0))

                def convolve(p, odd, first):
                    for g in range(2):
                        u = 2 * odd + g
                        at = (lambda base, n=1: bass.ds(p + base, n)) if not isinstance(p, int) else \
                            (lambda base, n=1: slice(p + base, p + base + n))
                        at2 = (lambda base: bass.ds(p * 2 + base, 2)) if not isinstance(p, int) else \
                            (lambda base: slice(p * 2 + base, p * 2 + base + 2))
                        w = [vec[:, at(V_CONV + j * 2 * FT + g * FT)] for j in range(3)]
                        cb = vec[:, at(V_CB + g * FT)]
                        k = 0 if first else 2
                        dve.wait_ge(up_copied, upto(l, up_copied, p * 2 + (g + 1)))
                        conv_link(V.tensor_copy(up[:, u, 2 + TP:4 + TP], vec[:, at2(V_ST + 2 * g * FT)]))
                        conv_link(V.tensor_scalar(conv[:, u, :], up[:, u, 0:CC], w[0], cb, ALU.mult, ALU.add))
                        conv_link(V.scalar_tensor_tensor(conv[:, u, :], up[:, u, 1:1 + CC], w[1], conv[:, u, :], ALU.mult, ALU.add))
                        V.tensor_copy(tail[:, at(g * FT), 0:2], up[:, u:u + 1, TP:TP + 2])
                        V.tensor_copy(tail[:, at(g * FT), 2:4], up[:, u:u + 1, UC - 2:UC])
                        V.scalar_tensor_tensor(conv[:, u, :], up[:, u, 2:2 + CC], w[2], conv[:, u, :], ALU.mult, ALU.add).then_inc(convolved, 1)

                def multiply(p, odd):
                    dve.wait_ge(silued, upto(l, silued, p + 1))
                    if not isinstance(p, int) or p >= 2:
                        dve.wait_ge(fal_ready, upto(l, fal_ready, p - 1))
                    dve.wait_ge(convolved, upto(l, convolved, p * 2 + 2))
                    V.tensor_tensor(prod[:, odd, :], sil[:, odd, :], conv[:, 2 * odd + 1, :], ALU.mult).then_inc(product_ready, 1)

                def product_low(p, odd):
                    dve.wait_ge(fah_ready, upto(l, fah_ready, p + 1))
                    o = (bass.ds(p, 1) if not isinstance(p, int) else slice(p, p + 1))
                    V.tensor_tensor(fal[:, o, :], prod[:, odd:odd + 1, :], fah[:, o, :].bitcast(F32), ALU.subtract).then_inc(fal_ready, 1)

                def conv_link(ins):
                    in_order(ins, conv_at[0])

                conv_at = [0]
                convolve(0, 0, True)
                convolve(1, 1, True)
                multiply(0, 0)
                with dve.Fori(0, FT // 2 - 1) as r:
                    conv_at[0] = r * CONV_LINKS
                    before = count[0]
                    for odd in range(2):
                        convolve(r * 2 + (2 + odd), odd, False)
                        product_low(r * 2 + odd, odd)
                        multiply(r * 2 + (1 + odd), 1 - odd)
                    assert count[0] - before == CONV_LINKS, count[0] - before
                count[0] += CONV_LINKS * (FT // 2 - 2)
                conv_at[0] = 0
                product_low(FT - 2, 0)
                multiply(FT - 1, 1)
                product_low(FT - 1, 1)

                with dve.Fori(0, 4) as r:
                    for b in range(2):
                        dve.wait_ge(piece_done, upto(l, piece_done, r * 6 + (done(Q_DOWN + 2) + 3 * b)))
                        for g, (a, n, c) in enumerate(((0, TP, 0), (TP, TS, TP + 2))):
                            i = V.scalar_tensor_tensor(
                                x[:, bass.ds(r * 2 + b, 1), a:a + n], ps[:, b:b + 1, c:c + n],
                                mod[:, bass.ds(r * 2 + (40 + b), 1), g],
                                x[:, bass.ds(r * 2 + b, 1), a:a + n], ALU.mult, ALU.add)
                        i.then_inc(bank_free[b], 1)
                dve.wait_ge(bank_free[0], taken(l, (2 * TILES2) // 2))
                dve.wait_ge(bank_free[1], taken(l, (2 * TILES2) // 2))
                assert count[0] == DVE_LINKS, ("DVE_LINKS", count[0])

            dve.wait_ge(fin[3], 1)
            count = [0]

            def link(ins):
                count[0] += 1
                ins.then_inc(fin[4], 1)
                dve.wait_ge(fin[4], count[0])

            newton(link, 1.0 / DM)
            link(V.tensor_tensor(work[:], x[:], rstd[:, 0:1, :].broadcast_to([P, KT, T]), ALU.mult))
            V.tensor_tensor(work[:], work[:], fg[:].unsqueeze(2).broadcast_to([P, KT, T]), ALU.mult).then_inc(y_ready, 1)


CONV_LINKS = 12
LINKS = (15, 253)


_OUTS = [("y_fm", (P, KT, T)), ("o_proj", (DEPTH, 6, P, 2, T)), ("o_ki", (DEPTH, IDX, T)), ("o_vb", (DEPTH, 2, P, TS)),
         ("o_logf", (DEPTH, NH, T)), ("o_conv", (DEPTH, P, 2 * FT, 4))]


def _constants(np):
    c = np.zeros((P, NCONST), np.float32)
    i, j = np.arange(P)[:, None], np.arange(P)[None, :]
    c[:, C_ID:C_ID + P] = i == j
    for at, width in ((C_PA, HD), (C_PI, IDX)):
        half = width // 2
        partner = j // width * width + (j % width + half) % width
        c[:, at:at + P] = i == partner
    c[:, C_ADM:C_ADM + P] = np.where((i < 64) & (j >= 64), INADMISSIBLE, 0)
    c[:, C_CAUSAL:C_CAUSAL + P] = np.where(j <= i, 0, MASKED)
    c[:, C_STRICT:C_STRICT + P] = np.where(i < j, 0, MASKED)
    c[:, C_STRICT1:C_STRICT1 + P] = i < j
    c[:, C_SPAT:C_SPAT + P] = i <= j
    c[:, C_NTRI:C_NTRI + P] = -(i >= j).astype(np.float32)
    c[:, C_NONE:C_NONE + P] = -1
    c[:, C_ONE:C_ONE + P] = 1
    c[0:TS, C_REP:C_REP + P] = (np.arange(TS)[:, None] == j % TS)
    pos = np.concatenate([np.arange(TP), PAST + np.arange(TS)]).astype(np.float32)
    for width, cos_at, sin_at in ((HD, C_COSA, C_SINA), (IDX, C_COSI, C_SINI)):
        half = width // 2
        inv = np.float32(10000.0) ** (-np.arange(half, dtype=np.float32) / np.float32(half))
        ang = inv[np.arange(P) % half][:, None] * pos[None, :]
        c[:, cos_at:cos_at + T] = np.cos(ang)
        c[:, sin_at:sin_at + T] = np.sin(ang) * np.where(np.arange(P) % width < half, -1, 1)[:, None]
    c[:, C_NEW:C_NEW + TS] = np.where(np.arange(TS)[None, :] <= np.arange(P)[:, None] % TS, 0, MASKED)
    c[:, C_QS:C_QS + NIN] = 1
    for t in (AQ, CQ, DQ):
        c[:, C_QS + t:C_QS + t + 2] = HD ** -0.5
    c[WROW:WROW + IH, C_QS + MISC] = (IDX * IH) ** -0.5
    c[:, C_EPS] = EPS
    c[4:8, C_FR], c[0:4, C_FR + 1] = 1, 1
    for h in range(NH):
        c[h, C_FL + 2 * h], c[4 + h, C_FL + 2 * h + 1] = 1, -1
    c[0:HD, C_HALF], c[HD:, C_HALF + 1] = 1, 1
    return c


def _layout(np, a):
    def fm(v):
        v = v.reshape(*v.shape[:-1], v.shape[-1] // P, P)
        return np.moveaxis(v, -1, 0)

    out = {}
    tokens = np.concatenate([a["x_prompt"][0], a["x_sample"][0]])
    out["x_fm"] = fm(tokens).transpose(0, 2, 1)
    mod = np.stack([w.reshape(4, 2, P, MOD_BLOCKS, 512).transpose(3, 0, 2, 1, 4).reshape(NMOD, P, PIECE)
                    for w in a["w_mod"]])
    out["mod_first"] = mod[0, :MOD_A]
    out["mod_vecs"] = np.stack([np.concatenate([fm(a["b_mod"][l]), fm(a["norm1_g"][l]), fm(a["norm2_g"][l])], axis=1)
                                for l in (*range(DEPTH), 0)], axis=1).reshape(P, -1)
    out["c_fm"] = fm(np.concatenate([a["c_prompt"], a["c_sample"]])).transpose(0, 2, 1)
    stream = np.zeros((DEPTH, NPIECE, P, PIECE), np.float32)

    def tiles_of(w):
        n = w.shape[1] // P
        return w.reshape(KT, P, n, P).transpose(2, 1, 0, 3).reshape(n, P, DM)

    widths = [256, 256, 256, 256, 32, 8, 256, 256, 256, 256, 256, 4, 256, 256, 256]
    at = np.concatenate([[0], np.cumsum(widths)])
    vecs = np.zeros((DEPTH, P, NVEC), np.float32)
    for l in range(DEPTH):
        (q, k, v, qi, ki, w, bu, bv, cq, ck, cv, cf, dq, dk, dv) = (
            a["w_in"][l][:, at[i]:at[i + 1]] for i in range(len(widths)))
        misc = np.zeros((DM, P), np.float32)
        misc[:, FROW:FROW + 4] = cf
        misc[:, FROW + 4:FROW + 8] = cf
        misc[:, WROW:WROW + IH] = w
        w_in = np.concatenate([q, k, v, qi, bu, bv, cq, ck, cv, dq, dk, dv, ki, ki, ki, ki, misc], axis=1)
        s = np.zeros((NSPLIT, P, PIECE), np.float32)
        s[Q_IN:Q_GATE] = tiles_of(w_in)
        s[Q_GATE:Q_BRANCH] = tiles_of(a["w_gate"][l])
        s[Q_BRANCH:Q_OUT] = a["w_branch"][l].reshape(4, 2, P, 2, 512).transpose(0, 3, 2, 1, 4).reshape(8, P, PIECE)
        s[Q_OUT:Q_UP] = tiles_of(a["w_out"][l])
        s[Q_UP:Q_DOWN].reshape(FT, 2, P, PIECE)[:, 0] = tiles_of(a["w_up"][l][:, :FF])
        s[Q_UP:Q_DOWN].reshape(FT, 2, P, PIECE)[:, 1] = tiles_of(a["w_up"][l][:, FF:])
        down = a["w_down"][l].reshape(FT, P, KT, P).transpose(2, 1, 0, 3)
        k0 = 0
        for c, n in enumerate(DOWN_SPLIT):
            s[Q_DOWN + c::3][:, :, :n * P] = down[:, :, k0:k0 + n].reshape(KT, P, n * P)
            k0 += n
        stream[l] = np.concatenate([s[:NIN], mod[l, MOD_A:], mod[(l + 1) % DEPTH, :MOD_A], s[NIN:]])
        v = vecs[l]
        v[:, V_LG:V_LG + 2] = fm(a["lnv_g"][l])
        v[:, V_LB:V_LB + 2] = fm(a["lnv_b"][l])
        v[:, V_GATE:V_GATE + 4 * KT] = fm(a["b_gate"][l])
        v[:, V_CONV:V_CB] = fm(a["w_conv"][l]).reshape(P, -1)
        v[:, V_CB:V_ST] = fm(a["b_conv"][l])
        v[:, V_ST:V_FB] = fm(a["state_ffn_conv"][l, 0]).transpose(0, 2, 1).reshape(P, -1)
        v[0:4, V_FB] = a["f_bias"][l]
        v[4:8, V_FB] = a["f_bias"][l]
        v[:, V_BS:V_BS + 2 * P] = np.repeat(a["b_spatial"][l].reshape(2, 2, P).transpose(1, 0, 2), 64, axis=0).reshape(P, 2 * P)
    out["stream"], out["vecs"], out["consts"] = stream, vecs, _constants(np)
    out["final_g"] = fm(a["final_g"])
    keys = np.stack([a["cache_a_k"], a["cache_c_k"], a["cache_d_k"]], axis=1)[:, :, 0]
    out["keys_t"] = keys.reshape(DEPTH, 3, PAST, 2, P).transpose(0, 1, 4, 3, 2)
    vals = np.stack([a["cache_a_v"], a["cache_c_v"], a["cache_d_v"]], axis=1)[:, :, 0]
    out["vals"] = vals.reshape(DEPTH, 3, 4, P, 256).transpose(0, 1, 3, 2, 4)
    ki_t = a["cache_a_kidx"][:, 0].transpose(0, 2, 1)
    out["kidx_t"] = np.concatenate([ki_t] * 4, axis=1)
    lp = a["cache_c_logf"][:, 0].transpose(0, 2, 1)
    out["logf_past"] = np.concatenate([lp, lp], axis=1)
    out["w_sp_t"] = a["w_spatial"].transpose(0, 3, 1, 2)
    return {k: np.ascontiguousarray(v) for k, v in out.items()}


def kernel(**inputs):
    import numpy as np
    import concourse.bacc as bacc
    from concourse.bass_utils import run_bass_kernel_spmd

    a = _layout(np, {k: np.asarray(v) for k, v in inputs.items()})
    nc = bacc.Bacc("TRN2", target_bir_lowering=False, num_devices=1)
    args = [nc.dram_tensor(k, v.shape, mybir.dt.from_np(v.dtype), kind="ExternalInput").ap() for k, v in a.items()]
    args += [nc.dram_tensor(n, shape, F32, kind="ExternalOutput").ap() for n, shape in _OUTS]
    encoder(nc, *args)
    r = run_bass_kernel_spmd(nc, [a], core_ids=[0]).results[0]

    y = r["y_fm"].transpose(2, 1, 0).reshape(T, DM)
    rows = r["o_proj"].transpose(1, 0, 4, 3, 2).reshape(6, DEPTH, T, NH, HD)
    split = lambda v: (np.ascontiguousarray(v[:, None, :TP]), np.ascontiguousarray(v[:, None, TP:]))
    ki = split(r["o_ki"].transpose(0, 2, 1))
    lf = split(r["o_logf"].transpose(0, 2, 1))
    vb = np.ascontiguousarray(r["o_vb"].transpose(0, 3, 1, 2).reshape(DEPTH, 1, TS, 2 * P))
    conv = r["o_conv"].transpose(0, 3, 2, 1).reshape(DEPTH, 1, 4, 2 * FF)
    ak, av, ck, cv, dk, dv = (split(rows[i]) for i in range(6))
    return (np.ascontiguousarray(y[None, :TP]), np.ascontiguousarray(y[None, TP:]), *ak, *av, *ki, vb, *ck, *cv, *lf, *dk, *dv,
            np.ascontiguousarray(conv[:, :, 0:2]), np.ascontiguousarray(conv[:, :, 2:4]))
```

```python
from contextlib import ExitStack

import concourse.bass as bass
from concourse import mybir

F32 = mybir.dt.float32
F32R = mybir.dt.float32r
ALU = mybir.AluOpType
ACT = mybir.ActivationFunctionType
X = mybir.AxisListType.X

P = 128
DM = 1024
DEPTH = 2
TP, TS = 256, 32
T = TP + TS
PAST = 512
HD = 64
NH = 4
IH = 8
IDX = 32
FF = 2816
KT = DM // P
FT = FF // P
SEL_P = (TP // 4) // 8
SEL_S = ((PAST + TS) // 4) // 8
EPS = 1e-6
MASKED = -1e30
INADMISSIBLE = -1e38
TAKEN = -3e38

AQI, AKI, MISC, BU, BV, DQ, DK, DV, AQ, AK, AV, CQ, CK, CV = 0, 2, 3, 4, 6, 8, 10, 12, 14, 16, 18, 20, 22, 24
NIN = 26
ROPED = (AQI, AQI + 1, AKI, AQ, AQ + 1, AK, AK + 1)
ROPED_EARLY = 3
DOTS_AT = 6
DOTS_PER = 3
B_MEAN_AT, B_VAR_AT, SWAP_Q_AT, B_TURN_AT, B_SPATIAL_AT, SWAP_K_AT = 14, 16, 18, 20, 22, 24
FROW, WROW = 0, 32

PIECE = 1024
NMOD = 48
MOD_A = 16
MOD_BLOCKS = NMOD // 4
FIRST_BLOCKS = MOD_A // 4
Q_IN, Q_GATE, Q_BRANCH, Q_OUT, Q_UP = 0, 26, 58, 66, 74
Q_DOWN = Q_UP + 2 * FT
DOWN_SPLIT = (8, 7, 7)
NSPLIT = Q_DOWN + KT * 3
NPIECE = NMOD + NSPLIT
RING = 4
AHEAD = 3

C_ID, C_ONE = 0, P
C_EPS = 2 * P
EARLY_CONST = 2 * P + 8
C_PA, C_PI, C_ADM, C_CAUSAL, C_STRICT, C_STRICT1, C_SPAT, C_NTRI, C_NONE, C_REP = (EARLY_CONST + P * i for i in range(10))
C_COSA = C_REP + P
C_SINA, C_COSI, C_SINI = C_COSA + T, C_COSA + 2 * T, C_COSA + 3 * T
C_NEW = C_COSA + 4 * T
C_QS = C_NEW + TS
C_FR = C_QS + NIN
C_FL = C_FR + 2
C_HALF = C_FL + 2 * NH
NCONST = C_HALF + 2

V_LG, V_LB = 0, 2
V_GATE = 4
V_CONV = V_GATE + 32
V_CB = V_CONV + 3 * 2 * FT
V_ST = V_CB + 2 * FT
V_FB = V_ST + 4 * FT
V_BS = V_FB + 1
NVEC = V_BS + 2 * P

M_MOD, M_G1, M_G2, NMV = 0, NMOD, NMOD + KT, NMOD + 2 * KT

N_PROJ_STORES = 10
UC = T + 4
CC = T + 2


def encoder(nc, x_fm, mod_first, mod_vecs, c_fm, stream, vecs, consts, final_g, keys_t, vals, kidx_t, logf_past, w_sp_t,
            y_fm, o_proj, o_ki, o_vb, o_logf, o_conv):
    with ExitStack() as ctx:
        top = [0]

        def place(name, shape, dt, at=None):
            size = 4
            for n in shape[1:]:
                size *= n
            size = (size + 31) // 32 * 32
            off = top[0] if at is None else at
            if at is None:
                top[0] = off + size
                assert top[0] <= 224 * 1024 - 64, (name, top[0])
            return nc.alloc_sbuf_tensor_at(name, shape, dt, offset=off), off, size

        base = (nc.sbuf_base + 31) // 32 * 32
        top[0] = base

        raw, _, _ = place("raw", [P, RING, PIECE], F32)
        whi, _, _ = place("whi", [P, RING, PIECE], F32R)
        wlo, _, _ = place("wlo", [P, RING, PIECE], F32R)
        cst, _, _ = place("cst", [P, NCONST], F32)
        vec, _, _ = place("vec", [P, NVEC], F32)
        x, _, _ = place("x", [P, KT, T], F32)
        work, work_at, _ = place("work", [P, KT, T], F32)
        hh, _, _ = place("hh", [P, KT, T], F32R)
        hl, _, _ = place("hl", [P, KT, T], F32R)
        oh, _, _ = place("oh", [P, KT, T], F32R)
        ol, _, _ = place("ol", [P, KT, T], F32R)
        proj, proj_at, proj_n = place("proj", [P, NIN, T], F32)
        gates, gates_at, gates_n = place("gates", [P, 4 * KT, T], F32)
        kv0k, kv0_at, _ = place("kv0k", [P, 2, PAST], F32)
        kv0v, _, _ = place("kv0v", [P, 4, 2 * P], F32)
        kv1k, _, _ = place("kv1k", [P, 2, PAST], F32)
        kv1v, _, _ = place("kv1v", [P, 4, 2 * P], F32)
        kix, _, _ = place("kix", [P, PAST], F32)
        wsp, _, _ = place("wsp", [P, 4, P], F32)
        fah, _, n = place("fah", [P, FT, CC], F32R, at=proj_at)
        fal, _, n2 = place("fal", [P, FT, CC], F32R, at=proj_at + n)
        assert n + n2 <= gates_at + gates_n - proj_at
        probs, _, n = place("probs", [P, 1024], F32, at=work_at)
        probs_t, _, n2 = place("probs_t", [P, 8, P], F32, at=work_at + n)
        relu, _, _ = place("relu", [P, DOTS_PER, 2 * T], F32, at=work_at)
        at = [gates_at]

        def scratch(name, shape):
            t, _, n = place(name, shape, F32, at=at[0])
            at[0] += n
            assert at[0] <= gates_at + gates_n, name
            return t

        d_keep = scratch("d_keep", [P, 2, 512])
        d_wt = scratch("d_wt", [P, 2, 512])
        vt = scratch("vt", [P, 3, 2 * P])
        scr = scratch("scr", [P, 2, 2 * T])
        queries = scr[:].rearrange("p a (b n) -> p (a b) n", b=2)
        score = scratch("score", [P, 3 * P + PAST + TS])
        fl8 = scratch("fl8", [8, NH, T])
        fcum_all = scratch("fcum", [P, TP + PAST + TS])
        fr_all = scratch("fr8", [P, TP + PAST + TS])
        fcum, fr8 = fcum_all[0:8], fr_all[0:8]
        mod_rows = [t[32:34, 0:512] for t in (fcum_all, fr_all)]
        lfp = scratch("lfp", [8, PAST])
        up, _, n = place("up", [P, 4, UC], F32, at=kv0_at)
        conv, _, n2 = place("conv", [P, 4, CC], F32, at=kv0_at + n)
        sil, _, n3 = place("sil", [P, 2, CC], F32, at=kv0_at + n + n2)
        prod, _, _ = place("prod", [P, 2, CC], F32, at=kv0_at + n + n2 + n3)

        lf, _, _ = place("lf", [8, T], F32)
        small, _, _ = place("small", [P, 64], F32)
        cmod, _, _ = place("cmod", [P, KT, 4], F32)
        mod, _, _ = place("mod", [P, NMOD, 2], F32)
        mvec, _, _ = place("mvec", [P, (DEPTH + 1) * NMV], F32)
        norm_a, _, _ = place("norm_a", [P, 2, KT, 2], F32)
        d_new, _, _ = place("d_new", [TS, 2, P], F32)
        tail, _, _ = place("tail", [P, 2 * FT, 4], F32)
        fg, _, _ = place("fg", [P, KT], F32)
        rstd, _, _ = place("rstd", [P, 2, T], F32)
        ctx.enter_context(nc.sbuf_tensor("fence", [P, top[0] - base + 64], mybir.dt.uint8))

        ps = ctx.enter_context(nc.psum_tensor("ps", [P, 8, 512], F32))
        flat = ps[:].rearrange("p b n -> p (b n)")

        def sem(name):
            return ctx.enter_context(nc.semaphore(name))

        per_layer = {}

        def signal(name, n):
            per_layer[name] = n
            return sem(name)

        raw_loaded = [sem(f"raw_loaded{s}") for s in range(RING)]
        raw_per_layer = [len(range(s, NPIECE, RING)) for s in range(RING)]
        bank_free = [sem(f"bank_free{b}") for b in range(2)]
        TILES2 = (NIN + 10 * KT) // 2
        start_loaded = sem("start_loaded")
        consts_loaded = sem("consts_loaded")
        y_stored = sem("y_stored")
        vecs_loaded = signal("vecs_loaded", 3 * 16)
        kix_loaded = signal("kix_loaded", 16)
        kv_d_loaded = signal("kv_d_loaded", 2 * 16)
        kv_c_loaded = signal("kv_c_loaded", 2 * 16)
        kv_a_loaded = signal("kv_a_loaded", 2 * 16)
        proj_stored = signal("proj_stored", N_PROJ_STORES * 16)
        tail_stored = signal("tail_stored", 16)
        mod_read = signal("mod_read", NMOD)
        hi_ready = signal("hi_ready", NSPLIT)
        lo_ready = signal("lo_ready", NSPLIT)
        piece_done = signal("piece_done", NSPLIT + 24)
        rows_taken = signal("rows_taken", MOD_BLOCKS)
        rows_turned = signal("rows_turned", MOD_BLOCKS)
        mod_ready = signal("mod_ready", MOD_BLOCKS)
        squared = signal("squared", 2 * KT)
        sums_ready = signal("sums_ready", 2)
        rstd_guess = signal("rstd_guess", 2)
        x_scaled = signal("x_scaled", 2 * KT)
        h_scaled = signal("h_scaled", 2 * KT)
        hh_ready = signal("hh_ready", 2 * KT)
        hl_ready = signal("hl_ready", 2 * KT)
        swapped = signal("swapped", 7)
        swap_read = signal("swap_read", 7)
        roped = signal("roped", 7)
        w_turned = signal("w_turned", 1)
        w_read = signal("w_read", 1)
        gelued = signal("gelued", 1)
        mean_ready = signal("mean_ready", 1)
        centred = signal("centred", 1)
        centred_squared = signal("centred_squared", 1)
        var_ready = signal("var_ready", 1)
        b_guess = signal("b_guess", 1)
        vb_ready = signal("vb_ready", 1)
        vb_turned = signal("vb_turned", 1)
        vb_tok = signal("vb_tok", 1)
        spatial_masked = signal("spatial_masked", 1)
        spatial_ready = signal("spatial_ready", 1)
        b_summed = signal("b_summed", 2)
        v_turned = signal("v_turned", 3)
        v_tok = signal("v_tok", 3)
        znew_ready = signal("znew_ready", 1)
        znew_log = signal("znew_log", 1)
        znew_keep = signal("znew_keep", 1)
        znew_logw = signal("znew_logw", 1)
        wnew_ready = signal("wnew_ready", 1)
        z_ready = signal("z_ready", NH)
        z_log = signal("z_log", NH)
        keep_ready = signal("keep_ready", NH)
        logw_ready = signal("logw_ready", NH)
        wt_ready = signal("wt_ready", NH)
        d_out = signal("d_out", NH)
        oh_ready = signal("oh_ready", 8)
        ol_ready = signal("ol_ready", 8)
        f_ready = signal("f_ready", 1)
        f_log = signal("f_log", 1)
        queries_ready = signal("queries_ready", 2)
        logits = signal("logits", 6)
        max_ready = signal("max_ready", 6)
        exp_ready = signal("exp_ready", 6)
        probs_ready = signal("probs_ready", 6)
        turned = signal("turned", 6)
        probs_tok = signal("probs_tok", 6)
        pv_done = signal("pv_done", 6)
        dots = signal("dots", 3 * IH)
        relued = signal("relued", 3 * IH)
        scored = signal("scored", 3 * IH)
        chosen = signal("chosen", 3)
        sigmoid_ready = signal("sigmoid_ready", 4)
        merged = signal("merged", KT)
        merged_h = signal("merged_h", KT)
        merged_l = signal("merged_l", KT)
        up_copied = signal("up_copied", 2 * FT)
        convolved = signal("convolved", 2 * FT)
        silued = signal("silued", FT)
        product_ready = signal("product_ready", FT)
        fah_ready = signal("fah_ready", FT)
        fal_ready = signal("fal_ready", FT)
        c_ready, c_exp, c_sig = sem("c_ready"), sem("c_exp"), sem("c_sig")
        y_ready = sem("y_ready")
        fin = [sem(f"final{i}") for i in range(6)]

        start_at = {"lo_ready": 1, "piece_done": 1, "tail_stored": 1}
        start_at["squared"] = KT
        start_at.update(mod_read=MOD_A, rows_taken=FIRST_BLOCKS, rows_turned=FIRST_BLOCKS,
                        mod_ready=FIRST_BLOCKS)
        settled = sem("settled")

        def upto(l, signal, k=None):
            n = per_layer[signal.name]
            return l * n + ((n if k is None else k) + start_at.get(signal.name, 0))

        def taken(l, tiles):
            return l * TILES2 + (tiles + 1)

        def loaded(l, slot, piece, more=0):
            return l * (16 * raw_per_layer[slot]) + (more + 16 * (MOD_A // RING + piece // RING + 1))

        def place_of(q):
            return q if q < NIN else q + NMOD

        ACT_LINKS, DVE_LINKS = LINKS
        act_own, dve_own = sem("act_own"), sem("dve_own")

        def done(q, j=0):
            if q < Q_BRANCH:
                return q + 1
            if q < Q_OUT:
                return Q_BRANCH + 4 * (q - Q_BRANCH) + j + 1
            return q + 1 + 24

        znew = ps[0:TS, 6:8, 0:2 * TS]

        def new_at(h):
            return (h % 2) * 2 * TS + (h // 2) * TS

        block = ctx.enter_context(nc.Block())

        @block.sync
        def _(sp):
            sp.dma_start(cst[:, 0:EARLY_CONST], consts[:, 0:EARLY_CONST]).then_inc(start_loaded, 16)
            sp.dma_start(x[:], x_fm).then_inc(start_loaded, 16)
            sp.dma_start(cmod[:, :, 0:2], c_fm).then_inc(start_loaded, 16)
            rounds = stream.rearrange("l (r s) p n -> l r s p n", s=2)
            sp.dma_start(mvec[:], mod_vecs).then_inc(start_loaded, 16)
            for i in range(MOD_A):
                if i >= RING:
                    sp.wait_ge(mod_read, i - RING + 1)
                sp.dma_start(raw[:, i % RING, :], mod_first[i]).then_inc(raw_loaded[i % RING], 16)
            sp.dma_start(cst[:, EARLY_CONST:], consts[:, EARLY_CONST:]).then_inc(consts_loaded, 16)
            sp.dma_start(fg[:], final_g).then_inc(consts_loaded, 16)
            with sp.Fori(0, DEPTH) as l:
                def load(pair, slot):
                    for j in range(2):
                        sp.dma_start(raw[:, slot + j, :], rounds[l, pair, j]).then_inc(raw_loaded[slot + j], 16)

                sp.wait_ge(mod_read, upto(l, mod_read, 0))
                for i in range(2):
                    sp.wait_ge(lo_ready, upto(l, lo_ready, 0))
                    load(i, 2 * i)
                sp.wait_ge(bank_free[0], taken(l, 0))
                sp.wait_ge(bank_free[1], taken(l, 0))
                sp.wait_ge(mod_ready, upto(l, mod_ready, 0))
                sp.dma_start(vec[:], vecs[l]).then_inc(vecs_loaded, 16)
                sp.dma_start(wsp[:], w_sp_t[l]).then_inc(vecs_loaded, 16)
                sp.dma_start(lfp[:], logf_past[l]).then_inc(vecs_loaded, 16)

                def split_pair(pair, at):
                    sp.wait_ge(lo_ready, upto(l, lo_ready, 2 * pair - 2))
                    load(at // 2 + pair, 2 * (pair % 2))

                def split_rounds(a, b, at):
                    with sp.Fori(0, (b - a) // 2) as r:
                        for i in range(2):
                            sp.wait_ge(lo_ready, upto(l, lo_ready, r * 4 + 2 * (a + i) - 2))
                            load(r * 2 + at // 2 + a + i, 2 * ((a + i) % 2))

                split_rounds(2, 4, 0)
                sp.dma_start(kix[:], kidx_t[l]).then_inc(kix_loaded, 16)
                sp.dma_start(kv0k[:], keys_t[l, 2]).then_inc(kv_d_loaded, 16)
                sp.dma_start(kv0v[:], vals[l, 2]).then_inc(kv_d_loaded, 16)
                sp.dma_start(kv1k[:], keys_t[l, 1]).then_inc(kv_c_loaded, 16)
                sp.dma_start(kv1v[:], vals[l, 1]).then_inc(kv_c_loaded, 16)
                split_rounds(4, 12, 0)
                split_pair(12, 0)
                for i in range(2):
                    sp.wait_ge(lo_ready, upto(l, lo_ready, NIN - 2 + 2 * i))
                    load(NIN // 2 + i, 2 * (1 - i))

                def mod_rounds(a, b):
                    with sp.Fori(0, (b - a) // 2) as r:
                        for i in range(2):
                            sp.wait_ge(mod_read, upto(l, mod_read, r * 4 + 2 * (a + i) - 2))
                            load(r * 2 + NIN // 2 + a + i, 2 * (1 - i))

                mod_rounds(2, 14)
                sp.wait_ge(d_out, upto(l, d_out))
                sp.sem_inc(settled, 1)
                sp.dma_start(kv0k[:], keys_t[l, 0]).then_inc(kv_a_loaded, 16)
                sp.dma_start(kv0v[:], vals[l, 0]).then_inc(kv_a_loaded, 16)
                mod_rounds(14, NMOD // 2)
                for i in range(2):
                    sp.wait_ge(mod_read, upto(l, mod_read, NMOD - 2 + 2 * i))
                    load((NIN + NMOD) // 2 + i, 2 * (1 - i))
                split_rounds(NIN // 2 + 2, 35, NMOD)
                sp.wait_ge(bank_free[0], taken(l, (NIN) // 2))
                sp.wait_ge(bank_free[1], taken(l, (NIN) // 2))
                sp.wait_ge(roped, upto(l, roped))
                sp.sem_inc(settled, 1)
                sp.wait_ge(vb_ready, upto(l, vb_ready))
                sp.wait_ge(f_ready, upto(l, f_ready))
                for i, t in enumerate((AK, AV, CK, CV, DK, DV)):
                    sp.dma_start(o_proj[l, i], proj[:, t:t + 2, :]).then_inc(proj_stored, 16)
                sp.dma_start(o_ki[l], proj[0:IDX, AKI, :]).then_inc(proj_stored, 16)
                sp.dma_start(o_vb[l, 0], proj[:, BV, TP:T]).then_inc(proj_stored, 16)
                sp.dma_start(o_vb[l, 1], proj[:, BV + 1, TP:T]).then_inc(proj_stored, 16)
                sp.dma_start(o_logf[l], lf[0:NH, :]).then_inc(proj_stored, 16)
                split_rounds(35, NSPLIT // 2, NMOD)
                sp.wait_ge(convolved, upto(l, convolved))
                sp.dma_start(o_conv[l], tail[:]).then_inc(tail_stored, 16)
            for k in range(0, KT, 2):
                sp.wait_ge(y_ready, k + 2)
                sp.dma_start(y_fm[:, k:k + 2, :], work[:, k:k + 2, :]).then_inc(y_stored, 16)
            sp.wait_ge(y_stored, 16 * KT // 2)
            sp.wait_ge(proj_stored, DEPTH * 16 * N_PROJ_STORES)
            sp.wait_ge(tail_stored, DEPTH * 16 + 1)

        @block.gpsimd
        def _(pool):
            for s in (*bank_free, lo_ready, piece_done, tail_stored):
                pool.sem_inc(s, 1)
            with pool.Fori(0, DEPTH) as l:
                def low(slot, q):
                    pool.wait_ge(hi_ready, upto(l, hi_ready, q + 1))
                    nc.gpsimd.tensor_tensor(wlo[:, slot, :], raw[:, slot, :], whi[:, slot, :].bitcast(F32),
                                                  ALU.subtract).then_inc(lo_ready, 1)

                def lows(a, b):
                    n = (b - a) // RING
                    if n:
                        with pool.Fori(0, n) as r:
                            for j in range(RING):
                                low((a + j) % RING, r * RING + (a + j))
                    for q in range(a + n * RING, b):
                        low(q % RING, q)

                def norm_low(n):
                    for k in range(KT):
                        pool.wait_ge(hh_ready, upto(l, hh_ready, (n - 1) * KT + k + 1))
                        nc.gpsimd.tensor_tensor(hl[:, k, :], work[:, k, :], hh[:, k, :].bitcast(F32),
                                                ALU.subtract).then_inc(hl_ready, 1)

                lows(Q_IN, Q_IN + AHEAD)
                norm_low(1)
                pool.sem_inc(settled, 1)
                lows(Q_IN + AHEAD, Q_UP + AHEAD)
                norm_low(2)
                pool.sem_inc(settled, 1)
                lows(Q_UP + AHEAD, NSPLIT)

        @block.tensor
        def _(pe):
            mm = nc.tensor.matmul
            ident = cst[:, C_ID:C_ID + P]

            def turn(out, in_):
                k = in_.shape[0]
                return mm(out, in_, ident[0:k, 0:k], start=True, stop=True, is_transpose=True)

            def mod_block(l, j):
                bank = j % 2
                if l is not None or j >= 2:
                    pe.wait_ge(mod_ready, j - 1 if l is None else upto(l, mod_ready, j - 1))
                for n in range(4):
                    slot = n if l is None else (NIN + n) % RING
                    pe.wait_ge(raw_loaded[slot], 16 * (j + 1) if l is None else loaded(l, slot, NIN + 4 * j + n))
                    for k in range(2):
                        i = mm(ps[32:34, bank, :], cmod[:, 2 * n + k, 2:4], raw[:, slot, k * 512:(k + 1) * 512],
                               start=(n + k == 0), stop=(n + k == 4))
                    i.then_inc(mod_read, 1)

            def mod_turn(l, j):
                pe.wait_ge(rows_taken, j + 1 if l is None else upto(l, rows_taken, j + 1))
                for m in range(4):
                    i = mm(ps[:, j % 2, 2 * m:2 * m + 2], mod_rows[j % 2][:, m * P:(m + 1) * P], ident[32:34, 32:34],
                           start=True, stop=True)
                i.then_inc(rows_turned, 1)

            def mod_step(l, j, blocks):
                if j < blocks:
                    mod_block(l, j)
                if 0 < j <= blocks:
                    mod_turn(l, j - 1)

            pe.wait_ge(c_sig, 1)
            pe.wait_ge(start_loaded, 16 * 4)
            for j in range(FIRST_BLOCKS + 1):
                mod_step(None, j, FIRST_BLOCKS)
            pe.wait_ge(consts_loaded, 16 * 2)
            with pe.Fori(0, DEPTH) as l:
                def sums(n):
                    for k in range(KT):
                        pe.wait_ge(squared, upto(l, squared, (n - 2) * KT + k + 1))
                        i = mm(ps[:, 7, 0:T], cst[:, C_ONE:C_ONE + P], work[:, k, :], start=(k == 0), stop=(k == KT - 1))
                    i.then_inc(sums_ready, 1)

                def product(out, slot, wcols, terms, ready=None, before=0):
                    n = len(terms)
                    for i, (k, high, low) in enumerate(terms):
                        if ready is not None:
                            pe.wait_ge(ready, upto(l, ready, before + i + 1))
                        a, b = k * P * wcols[0] + wcols[1] * P, k * P * wcols[0] + wcols[1] * P + P
                        mm(out, whi[:, slot, a:b], high, start=(i == 0 and wcols[2]), stop=False)
                        mm(out, whi[:, slot, a:b], low, start=False, stop=False)
                        last = mm(out, wlo[:, slot, a:b], high, start=False, stop=(i == n - 1 and wcols[3]))
                    return last

                h_terms = [(k, hh[:, k, :], hl[:, k, :]) for k in range(KT)]

                def tile_piece(slot, q, bank, tile2, ready=None):
                    pe.wait_ge(lo_ready, upto(l, lo_ready, q + 1))
                    pe.wait_ge(bank_free[bank], taken(l, tile2))
                    product(ps[:, bank, 0:T], slot, (1, 0, True, True), h_terms, ready).then_inc(piece_done, 1)

                def tiles(q0, n, tile0):
                    s0 = q0 % RING
                    if n >= RING:
                        with pe.Fori(0, n // RING) as r:
                            for j in range(RING):
                                tile_piece((s0 + j) % RING, r * RING + q0 + j, (tile0 + j) % 2, r * 2 + (tile0 + j) // 2)
                    for j in range(n - n % RING, n):
                        tile_piece((s0 + j) % RING, q0 + j, (tile0 + j) % 2, (tile0 + j) // 2)

                sums(1)
                pe.wait_ge(mod_ready, upto(l, mod_ready, 0))
                pe.sem_inc(settled, 1)

                def swap(n):
                    t = ROPED[n]
                    pe.wait_ge(bank_free[t % 2], taken(l, t // 2 + 1))
                    if n >= 2:
                        pe.wait_ge(swap_read, upto(l, swap_read, n - 1))
                    perm = C_PI if n < ROPED_EARLY else C_PA
                    mm(ps[:, 4 + n % 2, 0:T], cst[:, perm:perm + P], proj[:, t, :], start=True, stop=True).then_inc(swapped, 1)

                def index_dots(n):
                    c, h = n // IH, n % IH
                    if n >= DOTS_PER:
                        pe.wait_ge(relued, upto(l, relued, n - DOTS_PER + 1))
                    j, r, b = h // 4, 32 * (h % 4), 2 + 2 * (n % DOTS_PER)
                    if c < 2:
                        i = mm(ps[:, b, 0:(c + 1) * P], proj[r:r + 32, AQI + j, c * P:(c + 1) * P],
                               proj[r:r + 32, AKI, 0:(c + 1) * P], start=True, stop=True)
                    else:
                        if h == 0:
                            pe.wait_ge(kix_loaded, upto(l, kix_loaded))
                        pe.sem_inc(settled, 1)
                        q = proj[r:r + 32, AQI + j, TP:T]
                        mm(ps[0:TS, b, :], q, kix[r:r + 32, :], start=True, stop=True)
                        i = mm(ps[0:TS, b + 1, 0:TS], q, proj[r:r + 32, AKI, TP:T], start=True, stop=True)
                    i.then_inc(dots, 1)

                def turn_rows(t, turned_to):
                    for c, (a, n) in enumerate(((0, P), (P, P), (TP, TS))):
                        for j in range(2):
                            i = turn(ps[0:n, 4 + c // 2, (c % 2) * 256 + j * P:(c % 2) * 256 + (j + 1) * P],
                                     proj[:, t + j, a:a + n])
                    i.then_inc(turned_to, 1)

                for t in range(NIN):
                    tile_piece(t % RING, Q_IN + t, t % 2, t // 2, hl_ready if t == 0 else None)
                    if t == 4:
                        swap(0)
                        swap(1)
                    if t == 5:
                        swap(2)
                        pe.wait_ge(bank_free[MISC % 2], taken(l, MISC // 2 + 1))
                        pe.sem_inc(settled, 1)
                        for b, (a, n) in enumerate(((0, P), (P, P), (TP, TS))):
                            i = mm(ps[0:n, 7, 8 * b:8 * b + IH], proj[WROW:WROW + IH, MISC, a:a + n],
                                   ident[WROW:WROW + IH, WROW:WROW + IH], start=True, stop=True)
                        i.then_inc(w_turned, 1)
                    if t == DOTS_AT:
                        pe.wait_ge(roped, upto(l, roped, ROPED_EARLY))
                        pe.wait_ge(w_read, upto(l, w_read))
                        pe.sem_inc(settled, 1)
                    if DOTS_AT <= t < DOTS_AT + 3 * IH // DOTS_PER:
                        for n in range(DOTS_PER):
                            index_dots((t - DOTS_AT) * DOTS_PER + n)
                    if t == B_MEAN_AT:
                        pe.wait_ge(relued, upto(l, relued))
                        pe.wait_ge(gelued, upto(l, gelued))
                        for j in range(2):
                            i = mm(ps[:, 7, 0:T], cst[:, C_ONE:C_ONE + P], proj[:, BV + j, :], start=(j == 0), stop=(j == 1))
                        i.then_inc(mean_ready, 1)
                    if t == B_VAR_AT:
                        pe.wait_ge(centred_squared, upto(l, centred_squared))
                        for j in range(2):
                            i = mm(ps[:, 7, 0:T], cst[:, C_ONE:C_ONE + P], scr[:, j, 0:T], start=(j == 0), stop=(j == 1))
                        i.then_inc(var_ready, 1)
                    if t == SWAP_Q_AT:
                        swap(3)
                        swap(4)
                    if t == B_TURN_AT:
                        pe.wait_ge(swap_read, upto(l, swap_read, 5))
                        pe.wait_ge(vb_ready, upto(l, vb_ready))
                        turn_rows(BV, vb_turned)
                    if t == B_SPATIAL_AT:
                        pe.wait_ge(vb_tok, upto(l, vb_tok))
                        pe.wait_ge(spatial_masked, upto(l, spatial_masked))
                        for g in range(4):
                            r = 64 * (g % 2)
                            for c, (a, n) in enumerate(((0, P), (P, P), (TP, TS))):
                                i = mm(ps[r:r + 64, 6 + g // 2, a:a + n], vt[0:n, c, g * 64:(g + 1) * 64], wsp[0:n, g, 0:n],
                                       start=True, stop=True, skip_group_check=True)
                        i.then_inc(spatial_ready, 1)
                    if t == SWAP_K_AT:
                        swap(5)
                        swap(6)

                pe.wait_ge(bank_free[0], taken(l, (NIN) // 2))
                pe.wait_ge(bank_free[1], taken(l, (NIN) // 2))
                pe.wait_ge(swap_read, upto(l, swap_read))

                turn_rows(DV, v_turned)
                pe.wait_ge(kv_d_loaded, upto(l, kv_d_loaded))
                pe.wait_ge(b_summed, upto(l, b_summed))
                pe.sem_inc(settled, 1)
                for h in range(NH):
                    j, r = h // 2, 64 * (h % 2)
                    i = mm(ps[0:TS, 6 + h % 2, j * TS:(j + 1) * TS], proj[r:r + 64, DK + j, TP:T], proj[r:r + 64, DQ + j, TP:T],
                           start=(j == 0), stop=True, skip_group_check=True)
                i.then_inc(znew_ready, 1)

                def d_scores(h):
                    j, r, z = h // 2, 64 * (h % 2), 2 + h % 2
                    if h >= 2:
                        pe.wait_ge(wt_ready, upto(l, wt_ready, h - 1))
                    k, q = proj[r:r + 64, DK + j, :], proj[r:r + 64, DQ + j, :]
                    mm(ps[:, z, 0:TP], k[:, 0:P], q[:, 0:TP], start=True, stop=True, skip_group_check=True)
                    mm(ps[:, z, TP:3 * P], k[:, P:TP], q[:, P:TP], start=False, stop=True, skip_group_check=True)
                    for b in range(4):
                        i = mm(ps[:, z, 3 * P + b * TS:3 * P + (b + 1) * TS], kv0k[r:r + 64, j, b * P:(b + 1) * P],
                               q[:, TP:T], start=False, stop=True, skip_group_check=True)
                    i.then_inc(z_ready, 1)

                def d_log_weights(h):
                    z, b = 2 + h % 2, h % 2
                    pe.wait_ge(keep_ready, upto(l, keep_ready, h + 1))
                    ntri, nones = cst[:, C_NTRI:C_NTRI + P], cst[:, C_NONE:C_NONE + P]
                    kw = dict(start=False, stop=True, skip_group_check=True)
                    mm(ps[:, z, :], ntri, d_keep[:, b, :], **kw)
                    mm(ps[:, z, P:TP], nones, d_keep[:, b, TP:3 * P], **kw)
                    for c in range(1, 4):
                        src = d_keep[:, b, 3 * P + c * TS:3 * P + (c + 1) * TS].unsqueeze(1).broadcast_to([P, c, TS])
                        mm(ps[:, z, 3 * P:3 * P + c * TS].rearrange("p (c n) -> p c n", c=c), nones, src, **kw)
                    new = d_new[:, 0, new_at(h):new_at(h) + TS].unsqueeze(1).broadcast_to([TS, 4, TS])
                    mm(ps[:, z, 3 * P:4 * P].rearrange("p (c n) -> p c n", c=4), nones[0:TS, :], new, **kw).then_inc(logw_ready, 1)

                def d_values(h):
                    j, r, b = h // 2, 64 * (h % 2), h % 2
                    bank = 6 if j == 0 else 5
                    pe.wait_ge(wt_ready, upto(l, wt_ready, h + 1))
                    c = slice(h * 64, (h + 1) * 64)
                    kw = dict(skip_group_check=True)
                    mm(ps[r:r + 64, bank, 0:TP], vt[:, 0, c], d_wt[:, b, 0:TP], start=True, stop=False, **kw)
                    mm(ps[r:r + 64, bank, P:TP], vt[:, 1, c], d_wt[:, b, TP:3 * P], start=False, stop=True, **kw)
                    for k in range(4):
                        mm(ps[r:r + 64, bank, TP:T], kv0v[:, k, c], d_wt[:, b, 3 * P + k * TS:3 * P + (k + 1) * TS],
                           start=False, stop=False, **kw)
                    mm(ps[r:r + 64, bank, TP:T], vt[0:TS, 2, c], d_new[:, 1, new_at(h):new_at(h) + TS],
                             start=False, stop=True, **kw).then_inc(d_out, 1)

                d_scores(0)
                mod_step(l, 0, MOD_BLOCKS)
                pe.wait_ge(znew_keep, upto(l, znew_keep))
                pe.sem_inc(settled, 1)
                for b in range(2):
                    i = mm(ps[0:TS, 6 + b, 0:2 * TS], cst[0:TS, C_NTRI:C_NTRI + TS], d_new[:, 0, b * 64:(b + 1) * 64],
                           start=False, stop=True, skip_group_check=True)
                i.then_inc(znew_logw, 1)
                d_scores(1)
                mod_step(l, 1, MOD_BLOCKS)
                pe.wait_ge(v_tok, upto(l, v_tok, 1))
                pe.wait_ge(wnew_ready, upto(l, wnew_ready))
                for h in range(NH):
                    d_log_weights(h)
                    mod_step(l, 2 + h, MOD_BLOCKS)
                    d_values(h)
                    if h + 2 < NH:
                        d_scores(h + 2)

                def attention(n, k_t, kc, vc, forget):
                    for c in range(3):
                        u = 3 * n + c
                        nk, blocks = ((P, 1), (2 * P, 2), (PAST + TS, 5))[c]
                        if c == 0:
                            pe.wait_ge(v_tok, upto(l, v_tok, 2 + n))
                        if u:
                            pe.wait_ge(exp_ready, upto(l, exp_ready, u))
                        pe.wait_ge(queries_ready, upto(l, queries_ready, n + 1))
                        if n:
                            pe.wait_ge(chosen, upto(l, chosen, c + 1))
                        pe.sem_inc(settled, 1)
                        if c < 2:
                            per = 512 // nk
                            for h in range(NH):
                                o = flat[:, 1024 + h * nk:1024 + (h + 1) * nk]
                                i = mm(o, queries[:, h, c * P:(c + 1) * P], proj[:, k_t + h // 2, 0:nk],
                                       start=(h % per == 0), stop=(not forget), skip_group_check=True)
                                if forget:
                                    i = mm(o, fl8[:, h, c * P:(c + 1) * P], fr8[:, 0:nk], start=False, stop=True,
                                           skip_group_check=True)
                        else:
                            if not forget:
                                pe.wait_ge(kv_a_loaded, upto(l, kv_a_loaded))
                                rep = cst[0:TS, C_REP:C_REP + P]
                                mm(ps[:, 2, :], rep, score[0:TS, 3 * P:3 * P + PAST], start=True, stop=False, skip_group_check=True)
                                mm(ps[:, 3, 0:TS], rep, score[0:TS, 3 * P + PAST:3 * P + PAST + TS], start=True, stop=False,
                                   skip_group_check=True)
                            for h in range(NH):
                                j, o = h // 2, TS * h
                                q = queries[:, h, TP:T]
                                kw = dict(skip_group_check=True)
                                i = mm(ps[o:o + TS, 2, :], q, kc[:, j, :], start=forget, stop=(not forget), **kw)
                                i = mm(ps[o:o + TS, 3, 0:TS], q, proj[:, k_t + j, TP:T], start=forget,
                                       stop=(not forget), **kw)
                                if forget:
                                    mm(ps[o:o + TS, 2, :], fl8[:, h, TP:T], fr8[:, TP:TP + PAST], start=False, stop=True, **kw)
                                    i = mm(ps[o:o + TS, 3, 0:TS], fl8[:, h, TP:T], fr8[:, TP + PAST:], start=False,
                                           stop=True, **kw)
                        i.then_inc(logits, 1)
                        mod_step(l, 6 + u, MOD_BLOCKS)
                        pe.wait_ge(probs_ready, upto(l, probs_ready, u + 1))
                        if c < 2:
                            for h in range(NH):
                                for b in range(blocks):
                                    g = h * blocks + b
                                    i = turn(ps[:, 4 + g // 4, (g % 4) * P:(g % 4 + 1) * P],
                                             probs[:, g * P:(g + 1) * P])
                        else:
                            for b in range(4):
                                turn(ps[:, 4, b * P:(b + 1) * P], probs[:, b * P:(b + 1) * P])
                            i = turn(ps[0:TS, 5, 0:P], probs[:, PAST:PAST + TS])
                        i.then_inc(turned, 1)
                        if u == 5:
                            mod_step(l, MOD_BLOCKS, MOD_BLOCKS)
                        pe.wait_ge(probs_tok, upto(l, probs_tok, u + 1))
                        if c == 0:
                            pe.wait_ge(ol_ready, upto(l, ol_ready, 4 + 2 * n))
                        for h in range(NH):
                            j, r = h // 2, 64 * (h % 2)
                            v = slice(h * 64, (h + 1) * 64)
                            if c < 2:
                                for b in range(blocks):
                                    i = mm(ps[r:r + 64, 6 + j, c * P:(c + 1) * P], vt[:, b, v],
                                           probs_t[:, h * blocks + b, :], start=(b == 0), stop=(b == blocks - 1),
                                           skip_group_check=True)
                            else:
                                q = slice(h * TS, (h + 1) * TS)
                                for b in range(4):
                                    mm(ps[r:r + 64, 6 + j, TP:T], vc[:, b, v], probs_t[:, b, q], start=(b == 0),
                                       stop=False, skip_group_check=True)
                                i = mm(ps[r:r + 64, 6 + j, TP:T], vt[0:TS, 2, v], probs_t[0:TS, 4, q], start=False,
                                       stop=True, skip_group_check=True)
                        i.then_inc(pv_done, 1)

                pe.wait_ge(ol_ready, upto(l, ol_ready, 4))
                turn_rows(CV, v_turned)
                pe.wait_ge(f_ready, upto(l, f_ready))
                pe.wait_ge(kv_c_loaded, upto(l, kv_c_loaded))
                attention(0, CK, kv1k, kv1v, True)

                pe.wait_ge(probs_tok, upto(l, probs_tok, 3))
                pe.wait_ge(roped, upto(l, roped))
                turn_rows(AV, v_turned)
                attention(1, AK, kv0k, kv0v, False)

                pe.wait_ge(mod_ready, upto(l, mod_ready))
                pe.sem_inc(settled, 1)
                tiles(Q_GATE, 4 * KT, NIN)

                pe.wait_ge(ol_ready, upto(l, ol_ready))
                for p in range(8):
                    q, b = Q_BRANCH + p, p // 2
                    pe.wait_ge(lo_ready, upto(l, lo_ready, q + 1))
                    for m in range(4):
                        t = NIN + 4 * KT + 4 * p + m
                        pe.wait_ge(bank_free[t % 2], taken(l, t // 2))
                        terms = [(k, oh[:, 2 * b + k, :], ol[:, 2 * b + k, :]) for k in range(2)]
                        product(ps[:, t % 2, 0:T], q % RING, (4, m, True, True), terms).then_inc(piece_done, 1)

                tile_piece(Q_OUT % RING, Q_OUT, 0, (NIN + 8 * KT) // 2, merged_l)
                tiles(Q_OUT + 1, KT - 1, NIN + 8 * KT + 1)

                sums(2)

                def up_piece(slot, q, bank, copied, first=False):
                    pe.wait_ge(lo_ready, upto(l, lo_ready, q + 1))
                    if copied is None:
                        pe.wait_ge(bank_free[bank], taken(l, (NIN + 9 * KT) // 2))
                    else:
                        pe.wait_ge(up_copied, upto(l, up_copied, copied))
                    product(ps[:, bank, 0:T], slot, (1, 0, True, True), h_terms, hl_ready if first else None,
                            KT).then_inc(piece_done, 1)

                for j in range(RING):
                    up_piece((Q_UP + j) % RING, Q_UP + j, j % 2, None if j < 2 else j - 1, j == 0)
                with pe.Fori(0, 2 * FT // RING - 1) as r:
                    for j in range(RING):
                        up_piece((Q_UP + j) % RING, r * RING + (Q_UP + RING + j), j % 2, r * RING + (RING + j - 1))
                pe.wait_ge(up_copied, upto(l, up_copied))
                pe.sem_inc(settled, 1)
                with pe.Fori(0, 2) as r:
                    for m in range(4):
                        k0 = 0
                        t = NIN + 9 * KT + m
                        pe.wait_ge(bank_free[t % 2], taken(l, r * 2 + t // 2))
                        for c in range(3):
                            n = 3 * m + c
                            pe.wait_ge(lo_ready, upto(l, lo_ready, r * 12 + Q_DOWN + n + 1))
                            pe.wait_ge(fal_ready, upto(l, fal_ready, k0 + DOWN_SPLIT[c]))
                            terms = [(k, fah[:, k0 + k, :], fal[:, k0 + k, :]) for k in range(DOWN_SPLIT[c])]
                            product(ps[:, t % 2, 0:CC], (Q_DOWN + n) % RING, (1, 0, c == 0, c == 2), terms).then_inc(piece_done, 1)
                            k0 += DOWN_SPLIT[c]

            for k in range(KT):
                pe.wait_ge(squared, DEPTH * per_layer["squared"] + k + 1)
                i = mm(ps[:, 7, 0:T], cst[:, C_ONE:C_ONE + P], work[:, k, :], start=(k == 0), stop=(k == KT - 1))
            i.then_inc(fin[1], 1)

        @block.scalar
        def _(act):
            A = nc.scalar.activation
            eps = cst[:, C_EPS:C_EPS + 1]
            act.wait_ge(start_loaded, 16 * 4)
            A(cmod[:, :, 2:4], cmod[:, :, 0:2], ACT.Exp, scale=-1.0).then_inc(c_exp, 1)
            for k in range(KT):
                A(work[:, k, :], x[:, k, :], ACT.Square).then_inc(squared, 1)
            act.wait_ge(consts_loaded, 16 * 2)
            with act.Fori(0, DEPTH) as l:
                count = [0]

                def in_order(ins, at=0):
                    count[0] += 1
                    ins.then_inc(act_own, 1)
                    act.wait_ge(act_own, l * ACT_LINKS + (count[0] + at))

                def high(q, slot, first=False):
                    act.wait_ge(raw_loaded[slot], loaded(l, slot, place_of(q)))
                    if first:
                        act.wait_ge(piece_done, upto(l, piece_done, 0))
                    else:
                        act.wait_ge(piece_done, upto(l, piece_done, done(q - RING, 3)))
                    A(whi[:, slot, :], raw[:, slot, :], ACT.Copy).then_inc(hi_ready, 1)

                def high_in_loop(r, q, k, step):
                    slot = q % RING
                    act.wait_ge(raw_loaded[slot], loaded(l, slot, place_of(q), r * (16 * step // RING)))
                    act.wait_ge(piece_done, upto(l, piece_done, r * step + k))
                    A(whi[:, slot, :], raw[:, slot, :], ACT.Copy).then_inc(hi_ready, 1)

                def split_pieces(a, b):
                    for q in range(a, b):
                        if q + AHEAD < NSPLIT:
                            high(q + AHEAD, (q + AHEAD) % RING, q + AHEAD < RING)

                def split_loop(a, b):
                    n = (b - a) // RING
                    with act.Fori(0, n) as r:
                        for j in range(RING):
                            q = a + j + AHEAD
                            high_in_loop(r, q, done(q - RING, 3), RING)
                    split_pieces(a + n * RING, b)

                def square(m, tile):
                    act.wait_ge(bank_free[tile % 2], taken(l, tile // 2 + 1))
                    A(work[:, m, :], x[:, m, :], ACT.Square).then_inc(squared, 1)

                def norm(n):
                    act.wait_ge(sums_ready, upto(l, sums_ready, n))
                    in_order(A(rstd[:, 0, :], ps[:, 7, 0:T], ACT.Ln, scale=1.0 / DM, bias=eps))
                    A(rstd[:, 0, :], rstd[:, 0, :], ACT.Exp, scale=-0.5).then_inc(rstd_guess, 1)
                    if n == 1:
                        for q in range(AHEAD):
                            high(q, q, True)
                    for k in range(KT):
                        act.wait_ge(h_scaled, upto(l, h_scaled, (n - 1) * KT + k + 1))
                        A(hh[:, k, :], work[:, k, :], ACT.Copy).then_inc(hh_ready, 1)

                norm(1)
                def take_proj(t, bank):
                    act.wait_ge(piece_done, upto(l, piece_done, t + 1))
                    at = slice(t, t + 1) if isinstance(t, int) else bass.ds(t, 1)
                    scale = slice(t + C_QS, t + C_QS + 1) if isinstance(t, int) else bass.ds(t + C_QS, 1)
                    A(proj[:, at, :], ps[:, bank:bank + 1, 0:T], ACT.Copy, scale=cst[:, scale]).then_inc(bank_free[bank], 1)

                def rows_out(taken_out):
                    A(vt[:, 0:2, :], ps[:, 4, :].rearrange("p (c n) -> p c n", c=2), ACT.Copy)
                    A(vt[0:TS, 2, :], ps[0:TS, 5, 0:256], ACT.Copy).then_inc(taken_out, 1)

                for t in range(NIN):
                    if t + AHEAD < NIN:
                        high(t + AHEAD, (t + AHEAD) % RING, t + AHEAD < RING)
                    take_proj(t, t % 2)
                    for n in range(max(0, (t - DOTS_AT) * DOTS_PER), min(3 * IH, max(0, (t - DOTS_AT + 1) * DOTS_PER))):
                        c, b = n // IH, 1024 * (1 + n % DOTS_PER)
                        act.wait_ge(dots, upto(l, dots, n + 1))
                        if n >= DOTS_PER:
                            act.wait_ge(scored, upto(l, scored, n - DOTS_PER + 1))
                        if c < 2:
                            i = A(relu[:, n % DOTS_PER, 0:(c + 1) * P], flat[:, b:b + (c + 1) * P], ACT.Relu)
                        else:
                            i = A(relu[0:TS, n % DOTS_PER, 0:PAST + TS], flat[0:TS, b:b + PAST + TS], ACT.Relu)
                        i.then_inc(relued, 1)
                    if t == BV + 3:
                        act.wait_ge(bank_free[0], taken(l, (BV + 2) // 2))
                        act.wait_ge(bank_free[1], taken(l, (BV + 2) // 2))
                        A(proj[:, BU:BU + 4, :], proj[:, BU:BU + 4, :], ACT.Gelu_apprx_tanh).then_inc(gelued, 1)
                    if t == B_MEAN_AT + 1:
                        act.wait_ge(centred, upto(l, centred))
                        A(scr[:, :, 0:T], proj[:, BV:BV + 2, :], ACT.Square).then_inc(centred_squared, 1)
                    if t == B_VAR_AT + 1:
                        act.wait_ge(var_ready, upto(l, var_ready))
                        in_order(A(rstd[:, 0, :], ps[:, 7, 0:T], ACT.Ln, scale=1.0 / 256, bias=eps))
                        A(rstd[:, 0, :], rstd[:, 0, :], ACT.Exp, scale=-0.5).then_inc(b_guess, 1)
                        fx = fl8[:, 0, :]
                        act.wait_ge(vecs_loaded, upto(l, vecs_loaded))
                        in_order(A(fx, proj[FROW:FROW + 8, MISC, :], ACT.Abs, bias=vec[0:8, V_FB:V_FB + 1]))
                        in_order(A(fx, fx, ACT.Exp, scale=-1.0))
                        A(fx, fx, ACT.Ln, bias=1.0).then_inc(f_log, 1)
                    if t == B_TURN_AT + 1:
                        act.wait_ge(vb_turned, upto(l, vb_turned))
                        rows_out(vb_tok)
                for j in range(2):
                    act.wait_ge(b_summed, upto(l, b_summed, j + 1))
                    A(oh[:, 2 + j, :], scr[:, j, 0:T], ACT.Copy).then_inc(oh_ready, 1)

                act.wait_ge(v_turned, upto(l, v_turned, 1))
                act.wait_ge(spatial_ready, upto(l, spatial_ready))
                rows_out(v_tok)

                def soft_log(out, in_, logged):
                    in_order(A(out, in_, ACT.Abs))
                    in_order(A(out, out, ACT.Exp, scale=-1.0))
                    A(out, out, ACT.Ln, bias=1.0).then_inc(logged, 1)

                act.wait_ge(znew_ready, upto(l, znew_ready))
                soft_log(d_new[:, 0, :].rearrange("p (b n) -> p b n", b=2), znew, znew_log)
                for h in range(NH):
                    if h == 0:
                        act.wait_ge(z_ready, upto(l, z_ready, 1))
                        soft_log(d_keep[:, 0, :], ps[:, 2, :], z_log)
                        act.wait_ge(znew_logw, upto(l, znew_logw))
                        A(d_new[:, 1, :].rearrange("p (b n) -> p b n", b=2), znew, ACT.Exp).then_inc(wnew_ready, 1)
                    if h + 1 < NH:
                        act.wait_ge(z_ready, upto(l, z_ready, h + 2))
                        soft_log(d_keep[:, (h + 1) % 2, :], ps[:, 2 + (h + 1) % 2, :], z_log)
                    act.wait_ge(logw_ready, upto(l, logw_ready, h + 1))
                    if h >= 2:
                        act.wait_ge(d_out, upto(l, d_out, h - 1))
                    A(d_wt[:, h % 2, :], ps[:, 2 + h % 2, :], ACT.Exp).then_inc(wt_ready, 1)
                for j in range(2):
                    act.wait_ge(d_out, upto(l, d_out, 2 * j + 2))
                    A(oh[:, 6 + j, :], ps[:, 6 - j, 0:T], ACT.Copy).then_inc(oh_ready, 1)

                def softmaxes(n):
                    for c in range(3):
                        u = 3 * n + c
                        act.wait_ge(max_ready, upto(l, max_ready, u + 1))
                        if u:
                            act.wait_ge(turned, upto(l, turned, u))
                        if c < 2:
                            nk = (c + 1) * P
                            for h in range(NH):
                                i = A(probs[:, h * nk:(h + 1) * nk], flat[:, 1024 + h * nk:1024 + (h + 1) * nk], ACT.Exp,
                                      bias=small[:, h:h + 1], accum_out=small[:, 8 + h:9 + h])
                        else:
                            i = A(probs[:, 0:PAST + TS], flat[:, 1024:1024 + PAST + TS], ACT.Exp,
                                  bias=small[:, 0:1], accum_out=small[:, 8:9])
                        i.then_inc(exp_ready, 1)
                        act.wait_ge(turned, upto(l, turned, u + 1))
                        if u:
                            act.wait_ge(pv_done, upto(l, pv_done, u))
                        if c == 0:
                            i = A(probs_t[:, 0:4, :], ps[:, 4, :].rearrange("p (c n) -> p c n", c=4), ACT.Copy)
                        elif c == 1:
                            i = A(probs_t[:], ps[:, 4:6, :].rearrange("p b (c n) -> p (b c) n", c=4), ACT.Copy)
                        else:
                            A(probs_t[:, 0:4, :], ps[:, 4, :].rearrange("p (c n) -> p c n", c=4), ACT.Copy)
                            i = A(probs_t[0:TS, 4, :], ps[0:TS, 5, 0:P], ACT.Copy)
                        i.then_inc(probs_tok, 1)
                    if n == 1:
                        split_pieces(NIN - AHEAD, NIN)
                    act.wait_ge(pv_done, upto(l, pv_done, 3 * n + 3))
                    for j in range(2):
                        A(oh[:, 4 * (1 - n) + j, :], ps[:, 6 + j, 0:T], ACT.Copy).then_inc(oh_ready, 1)

                act.wait_ge(v_turned, upto(l, v_turned, 2))
                act.wait_ge(d_out, upto(l, d_out))
                rows_out(v_tok)
                softmaxes(0)

                act.wait_ge(v_turned, upto(l, v_turned, 3))
                act.wait_ge(pv_done, upto(l, pv_done, 3))
                rows_out(v_tok)
                softmaxes(1)

                split_loop(Q_GATE, Q_BRANCH)
                for b in range(4):
                    act.wait_ge(bank_free[0], taken(l, (NIN + (b + 1) * KT) // 2))
                    act.wait_ge(bank_free[1], taken(l, (NIN + (b + 1) * KT) // 2))
                    A(gates[:, b * KT:(b + 1) * KT, :], gates[:, b * KT:(b + 1) * KT, :], ACT.Sigmoid).then_inc(sigmoid_ready, 1)
                split_pieces(Q_BRANCH, Q_OUT)
                for m in range(KT):
                    act.wait_ge(merged, upto(l, merged, m + 1))
                    A(hh[:, m, :], work[:, m, :], ACT.Copy).then_inc(merged_h, 1)
                for m in range(KT):
                    high(Q_OUT + m + AHEAD, (Q_OUT + m + AHEAD) % RING)
                    if m:
                        square(m - 1, NIN + 8 * KT + m - 1)
                square(KT - 1, NIN + 9 * KT - 1)
                norm(2)

                def up_pair(p, odd, r=None):
                    for g in range(2):
                        u = 2 * odd + g
                        if r is None:
                            q = Q_UP + 2 * p + g + AHEAD
                            if q < NSPLIT:
                                high(q, q % RING)
                        else:
                            q = Q_UP + 2 * odd + 4 + g + AHEAD
                            high_in_loop(r, q, done(q - RING), RING)
                        act.wait_ge(piece_done, upto(l, piece_done, p * 2 + (done(Q_UP) + g)))
                        if r is not None or p >= 2:
                            act.wait_ge(convolved, upto(l, convolved, p * 2 + (g - 3)))
                        elif p == 0 and g == 0:
                            act.wait_ge(ol_ready, upto(l, ol_ready))
                        A(up[:, u, 2:2 + TP], ps[:, g, 0:TP], ACT.Copy)
                        A(up[:, u, 4 + TP:4 + T], ps[:, g, TP:T], ACT.Copy).then_inc(up_copied, 1)

                def silu(p, odd):
                    act.wait_ge(convolved, upto(l, convolved, p * 2 + 2))
                    A(sil[:, odd, :], conv[:, 2 * odd, :], ACT.Silu).then_inc(silued, 1)

                def product_high(p, odd):
                    act.wait_ge(product_ready, upto(l, product_ready, p + 1))
                    A(fah[:, bass.ds(p, 1), :] if not isinstance(p, int) else fah[:, p:p + 1, :],
                            prod[:, odd:odd + 1, :], ACT.Copy).then_inc(fah_ready, 1)

                act.wait_ge(proj_stored, upto(l, proj_stored))
                up_pair(0, 0)
                up_pair(1, 1)
                silu(0, 0)
                with act.Fori(0, FT // 2 - 1) as r:
                    for odd in range(2):
                        p = r * 2 + (2 + odd)
                        up_pair(p, odd, r)
                        product_high(r * 2 + odd, odd)
                        silu(r * 2 + (1 + odd), 1 - odd)
                product_high(FT - 2, 0)
                silu(FT - 1, 1)
                product_high(FT - 1, 1)
                for m in range(KT):
                    split_pieces(Q_DOWN + 3 * m, Q_DOWN + 3 * m + 2)
                    if m:
                        square(m - 1, NIN + 9 * KT + m - 1)
                    split_pieces(Q_DOWN + 3 * m + 2, Q_DOWN + 3 * m + 3)
                square(KT - 1, NIN + 10 * KT - 1)
                assert count[0] == ACT_LINKS, ("ACT_LINKS", count[0])

            act.wait_ge(fin[1], 1)
            A(rstd[:, 0, :], ps[:, 7, 0:T], ACT.Ln, scale=1.0 / DM, bias=eps).then_inc(fin[2], 1)
            act.wait_ge(fin[2], 1)
            A(rstd[:, 0, :], rstd[:, 0, :], ACT.Exp, scale=-0.5).then_inc(fin[3], 1)

        @block.vector
        def _(dve):
            V = nc.vector
            dve.wait_ge(start_loaded, 16 * 4)
            dve.wait_ge(c_exp, 1)
            cs = cmod[:, :, 2:4]
            V.tensor_scalar(cs, cs, 1.0, None, ALU.add).then_inc(c_ready, 1)
            dve.wait_ge(c_ready, 1)
            V.reciprocal(cs, cs).then_inc(c_ready, 1)
            dve.wait_ge(c_ready, 2)
            V.tensor_tensor(cs, cs, cmod[:, :, 0:2], ALU.mult).then_inc(c_sig, 1)

            def newton(link, n):
                y, v = rstd[:, 0, :], rstd[:, 1, :]
                link(V.scalar_tensor_tensor(v, ps[:, 7, 0:T], n * EPS, y, ALU.add, ALU.mult))
                link(V.scalar_tensor_tensor(v, v, -0.5 / n, y, ALU.mult, ALU.mult))
                link(V.scalar_tensor_tensor(y, v, 1.5, y, ALU.add, ALU.mult))

            def mod_take(l, j):
                dve.wait_ge(mod_read, 4 * j + 4 if l is None else upto(l, mod_read, 4 * j + 4))
                V.tensor_copy(mod_rows[j % 2], ps[32:34, j % 2, :]).then_inc(rows_taken, 1)

            def mod_add(l, j):
                dve.wait_ge(rows_turned, j + 1 if l is None else upto(l, rows_turned, j + 1))
                if l is None:
                    m, at = 4 * j, slice(4 * j, 4 * j + 4)
                else:
                    m = (MOD_A + 4 * j) % NMOD
                    at = bass.ds(l * NMV + (m if m >= MOD_A else NMV + m), 4)
                V.tensor_tensor(mod[:, m:m + 4, :], ps[:, j % 2, 0:8].rearrange("p (m g) -> p m g", g=2),
                                mvec[:, at].unsqueeze(2).broadcast_to([P, 4, 2]), ALU.add).then_inc(mod_ready, 1)

            def mod_step(l, j, blocks):
                if 2 <= j < blocks + 2:
                    mod_add(l, j - 2)
                if 1 <= j < blocks + 1:
                    mod_take(l, j - 1)

            def norm_scale(link, n, scale_at, g_at):
                link(V.tensor_scalar(norm_a[:, n], mod[:, scale_at:scale_at + KT, :], 1.0, None, ALU.add))
                link(V.tensor_tensor(norm_a[:, n], norm_a[:, n], mvec[:, g_at].unsqueeze(2).broadcast_to([P, KT, 2]), ALU.mult))

            for j in range(FIRST_BLOCKS + 2):
                mod_step(None, j, FIRST_BLOCKS)
            dve.wait_ge(mod_ready, FIRST_BLOCKS)
            links = [2]

            def first_link(ins):
                links[0] += 1
                ins.then_inc(c_ready, 1)
                dve.wait_ge(c_ready, links[0])

            norm_scale(first_link, 0, KT, slice(M_G1, M_G1 + KT))

            dve.wait_ge(consts_loaded, 16 * 2)
            with dve.Fori(0, DEPTH) as l:
                count = [0]

                def in_order(ins, at=0):
                    count[0] += 1
                    ins.then_inc(dve_own, 1)
                    dve.wait_ge(dve_own, l * DVE_LINKS + (count[0] + at))

                dve.wait_ge(vecs_loaded, upto(l, vecs_loaded))
                V.tensor_tensor(wsp[:], wsp[:], cst[:, C_SPAT:C_SPAT + P].unsqueeze(1).broadcast_to([P, 4, P]), ALU.mult).then_inc(spatial_masked, 1)

                def norm(n):
                    shift_at = 0 if n == 1 else 24
                    dve.wait_ge(rstd_guess, upto(l, rstd_guess, n))
                    newton(in_order, DM)
                    at = (n - 1) * KT
                    for k in range(KT + 1):
                        if k < KT:
                            V.tensor_tensor(work[:, k, :], x[:, k, :], rstd[:, 0, :], ALU.mult).then_inc(x_scaled, 1)
                        if k:
                            dve.wait_ge(x_scaled, upto(l, x_scaled, at + k))
                            for g, (a, b) in enumerate(((0, TP), (TP, T))):
                                i = V.tensor_scalar(work[:, k - 1, a:b], work[:, k - 1, a:b], norm_a[:, n - 1, k - 1, g:g + 1],
                                                    mod[:, shift_at + k - 1, g:g + 1], ALU.mult, ALU.add)
                            i.then_inc(h_scaled, 1)

                norm(1)

                def rotate(n):
                    t = ROPED[n]
                    cos, sin = (C_COSI, C_SINI) if n < ROPED_EARLY else (C_COSA, C_SINA)
                    dve.wait_ge(swapped, upto(l, swapped, n + 1))
                    if n >= 2:
                        dve.wait_ge(roped, upto(l, roped, n - 1))
                    V.tensor_tensor(scr[:, n % 2, 0:T], ps[:, 4 + n % 2, 0:T], cst[:, sin:sin + T], ALU.mult).then_inc(swap_read, 1)
                    dve.wait_ge(swap_read, upto(l, swap_read, n + 1))
                    in_order(V.tensor_tensor(proj[:, t, :], proj[:, t, :], cst[:, cos:cos + T], ALU.mult))
                    V.tensor_tensor(proj[:, t, :], proj[:, t, :], scr[:, n % 2, 0:T], ALU.add).then_inc(roped, 1)

                for n in range(ROPED_EARLY):
                    rotate(n)
                dve.wait_ge(w_turned, upto(l, w_turned))
                V.tensor_copy(small[:, 16:32], ps[:, 7, 0:16])
                V.tensor_copy(small[0:TS, 32:40], ps[0:TS, 7, 16:24]).then_inc(w_read, 1)
                dve.wait_ge(w_read, upto(l, w_read))

                parts = ((0, P, P), (P, 2 * P, P), (3 * P, PAST + TS, TS))
                for c, (a, nk, m) in enumerate(parts):
                    s = score[0:m, a:a + nk]
                    for h in range(IH):
                        n = c * IH + h
                        w = small[0:m, 16 + 8 * c + h:17 + 8 * c + h]
                        dve.wait_ge(relued, upto(l, relued, n + 1))
                        if h == 0:
                            i = V.tensor_scalar(s, relu[0:m, n % DOTS_PER, 0:nk], w, None, ALU.mult)
                        else:
                            i = V.scalar_tensor_tensor(s, relu[0:m, n % DOTS_PER, 0:nk], w, s, ALU.mult, ALU.add)
                        i.then_inc(scored, 1)
                        dve.wait_ge(scored, upto(l, scored, n + 1))
                    if c < 2:
                        d = score[:, a + c * P:a + (c + 1) * P]
                        in_order(V.tensor_tensor(d, d, cst[:, C_ADM:C_ADM + P], ALU.add))
                def choose(c, rounds, last=True):
                    a, nk, m = parts[c]
                    s = score[0:m, a:a + nk]
                    best = small[0:m, 40:48]
                    for _ in range(rounds):
                        dve.sem_inc(settled, 1)
                        in_order(V.max(best, s))
                        dve.sem_inc(settled, 1)
                        in_order(V.match_replace(s, best, s, TAKEN))
                    if last:
                        V.tensor_scalar(s, s, 0.5 * (TAKEN + INADMISSIBLE), MASKED, ALU.is_gt, ALU.mult).then_inc(chosen, 1)

                dve.wait_ge(mean_ready, upto(l, mean_ready))
                for j in range(2):
                    i = V.scalar_tensor_tensor(proj[:, BV + j, :], ps[:, 7, 0:T], -1.0 / 256, proj[:, BV + j, :], ALU.mult, ALU.add)
                i.then_inc(centred, 1)
                choose(0, SEL_P)
                dve.wait_ge(b_guess, upto(l, b_guess))
                newton(in_order, 256)
                in_order(V.tensor_tensor(proj[:, BV:BV + 2, :], proj[:, BV:BV + 2, :],
                                       rstd[:, 0:1, :].broadcast_to([P, 2, T]), ALU.mult))
                for j in range(2):
                    i = V.tensor_scalar(proj[:, BV + j, :], proj[:, BV + j, :], vec[:, V_LG + j:V_LG + j + 1],
                                        vec[:, V_LB + j:V_LB + j + 1], ALU.mult, ALU.add)
                i.then_inc(vb_ready, 1)
                rotate(3)
                rotate(4)
                in_order(V.tensor_scalar(lf[:], proj[FROW:FROW + 8, MISC, :], vec[0:8, V_FB:V_FB + 1], 0.0, ALU.add, ALU.min))
                dve.wait_ge(f_log, upto(l, f_log))
                ones8 = lambda n: cst[0:8, C_ONE:C_ONE + 1].broadcast_to([8, n])
                in_order(V.tensor_tensor(lf[:], lf[:], fl8[:, 0, :], ALU.subtract))
                in_order(V.tensor_tensor_scan(fcum[:, 0:TP], ones8(TP), lf[:, 0:TP], 0.0, ALU.mult, ALU.add))
                in_order(V.tensor_tensor_scan(fcum[:, TP:TP + PAST], ones8(PAST), lfp[:], 0.0, ALU.mult, ALU.add))
                in_order(V.tensor_tensor_scan(fcum[:, TP + PAST:], ones8(TS), lf[:, TP:T],
                                            fcum[:, TP + PAST - 1:TP + PAST], ALU.mult, ALU.add))
                V.tensor_scalar(fr8[:], fcum[:], cst[0:8, C_FR:C_FR + 1], cst[0:8, C_FR + 1:C_FR + 2], ALU.mult, ALU.add)
                for h in range(NH):
                    a, b = (cst[0:8, C_FL + 2 * h + i:C_FL + 2 * h + i + 1] for i in range(2))
                    V.tensor_scalar(fl8[:, h, 0:TP], fcum[:, 0:TP], a, b, ALU.mult, ALU.add)
                    i = V.tensor_scalar(fl8[:, h, TP:T], fcum[:, TP + PAST:], a, b, ALU.mult, ALU.add)
                i.then_inc(f_ready, 1)

                rotate(5)
                rotate(6)
                dve.wait_ge(roped, upto(l, roped))
                dve.wait_ge(spatial_ready, upto(l, spatial_ready))
                for j in range(2):
                    bs = vec[:, V_BS + j * P:V_BS + (j + 1) * P]
                    V.tensor_tensor(scr[:, j, 0:TP].rearrange("p (c n) -> p c n", c=2),
                                    ps[:, 6 + j, 0:TP].rearrange("p (c n) -> p c n", c=2),
                                    bs.unsqueeze(1).broadcast_to([P, 2, P]), ALU.add)
                    in_order(V.tensor_tensor(scr[:, j, TP:T], ps[:, 6 + j, TP:T], bs[:, 0:TS], ALU.add))
                    V.tensor_tensor(scr[:, j, 0:T], scr[:, j, 0:T], proj[:, BU + j, :], ALU.mult).then_inc(b_summed, 1)
                for j in range(2):
                    dve.wait_ge(oh_ready, upto(l, oh_ready, j + 1))
                    V.tensor_tensor(ol[:, 2 + j, :], scr[:, j, 0:T], oh[:, 2 + j, :].bitcast(F32), ALU.subtract).then_inc(ol_ready, 1)

                strict, strict1 = cst[:, C_STRICT:C_STRICT + P], cst[:, C_STRICT1:C_STRICT1 + P]
                dve.wait_ge(znew_log, upto(l, znew_log))
                keep = d_new[:, 0, :].rearrange("p (b n) -> p b n", b=2)
                in_order(V.scalar_tensor_tensor(keep, znew, 0.0, keep, ALU.max, ALU.add))
                n4 = lambda ap: ap.rearrange("p (h n) -> p h n", h=NH)
                z4 = znew.rearrange("p b (j n) -> p b j n", j=2)
                V.tensor_tensor(z4, z4, strict[0:TS, 0:TS].unsqueeze(1).unsqueeze(1).broadcast_to([TS, 2, 2, TS]), ALU.add)
                V.tensor_tensor(n4(d_new[:, 0, :]), n4(d_new[:, 0, :]),
                                      strict1[0:TS, 0:TS].unsqueeze(1).broadcast_to([TS, NH, TS]), ALU.mult).then_inc(znew_keep, 1)
                mod_step(l, 1, MOD_BLOCKS)
                for h in range(NH):
                    b = h % 2
                    z = ps[:, 2 + b, :]
                    diag = lambda ap: ap.rearrange("p (a n) -> p a n", n=P)[:, 0:3:2, :]
                    dve.wait_ge(z_log, upto(l, z_log, h + 1))
                    in_order(V.scalar_tensor_tensor(d_keep[:, b, :], z, 0.0, d_keep[:, b, :], ALU.max, ALU.add))
                    V.tensor_tensor(diag(z), diag(z), strict.unsqueeze(1).broadcast_to([P, 2, P]), ALU.add)
                    V.tensor_tensor(diag(d_keep[:, b, :]), diag(d_keep[:, b, :]),
                                          strict1.unsqueeze(1).broadcast_to([P, 2, P]), ALU.mult).then_inc(keep_ready, 1)
                    mod_step(l, 2 + h, MOD_BLOCKS)
                    choose(1, SEL_P // NH, h == NH - 1)
                for j in range(2):
                    dve.wait_ge(oh_ready, upto(l, oh_ready, 3 + j))
                    V.tensor_tensor(ol[:, 6 + j, :], ps[:, 6 - j, 0:T], oh[:, 6 + j, :].bitcast(F32), ALU.subtract).then_inc(ol_ready, 1)

                def softmaxes(n, q_t):
                    for h in range(NH):
                        i = V.tensor_scalar(queries[:, h, :], proj[:, q_t + h // 2, :],
                                            cst[:, C_HALF + h % 2:C_HALF + h % 2 + 1], None, ALU.mult)
                    i.then_inc(queries_ready, 1)
                    for c in range(3):
                        u = 3 * n + c
                        nk = (P, 2 * P, PAST + TS)[c]
                        if n:
                            dve.wait_ge(chosen, upto(l, chosen, c + 1))
                        mod_step(l, 6 + u, MOD_BLOCKS)
                        dve.wait_ge(logits, upto(l, logits, u + 1))
                        if c < 2:
                            lg = flat[:, 1024:1024 + NH * nk].rearrange("p (h k) -> p h k", h=NH)
                            if n == 0:
                                d = lg[:, :, c * P:(c + 1) * P]
                                in_order(V.tensor_tensor(d, d, cst[:, C_CAUSAL:C_CAUSAL + P].unsqueeze(1).broadcast_to([P, NH, P]), ALU.add))
                            else:
                                m = score[:, c * P:c * P + nk]
                                in_order(V.tensor_tensor(lg, lg, m.unsqueeze(1).broadcast_to([P, NH, nk]), ALU.add))
                            V.tensor_reduce(small[:, 0:NH], lg, X, ALU.max, negate=True).then_inc(max_ready, 1)
                        else:
                            lg = flat[:, 1024:1024 + nk]
                            if n == 0:
                                in_order(V.tensor_tensor(lg[:, PAST:], lg[:, PAST:], cst[:, C_NEW:C_NEW + TS], ALU.add))
                            V.tensor_reduce(small[:, 0:1], lg, X, ALU.max, negate=True).then_inc(max_ready, 1)
                        dve.wait_ge(exp_ready, upto(l, exp_ready, u + 1))
                        if c < 2:
                            in_order(V.reciprocal(small[:, 12:12 + NH], small[:, 8:8 + NH]))
                            e = probs[:, 0:NH * nk].rearrange("p (h k) -> p h k", h=NH)
                            i = V.tensor_tensor(e, e, small[:, 12:12 + NH].unsqueeze(2).broadcast_to([P, NH, nk]), ALU.mult)
                        else:
                            in_order(V.reciprocal(small[:, 12:13], small[:, 8:9]))
                            i = V.tensor_scalar(probs[:, 0:nk], probs[:, 0:nk], small[:, 12:13], None, ALU.mult)
                        i.then_inc(probs_ready, 1)
                        if u < 5:
                            choose(2, (SEL_S + u) // 5, u == 4)
                        if u == 5:
                            mod_step(l, MOD_BLOCKS, MOD_BLOCKS)
                    for j in range(2):
                        dve.wait_ge(oh_ready, upto(l, oh_ready, 5 + 2 * n + j))
                        t = 4 * (1 - n) + j
                        V.tensor_tensor(ol[:, t, :], ps[:, 6 + j, 0:T], oh[:, t, :].bitcast(F32), ALU.subtract).then_inc(ol_ready, 1)

                assert sum((SEL_S + u) // 5 for u in range(5)) == SEL_S and SEL_P % NH == 0
                softmaxes(0, CQ)

                softmaxes(1, AQ)
                mod_step(l, MOD_BLOCKS + 1, MOD_BLOCKS)
                dve.wait_ge(mod_ready, upto(l, mod_ready))
                norm_scale(in_order, 0, KT, bass.ds(l * NMV + (NMV + M_G1), KT))
                norm_scale(in_order, 1, 4 * KT, bass.ds(l * NMV + M_G2, KT))

                dve.sem_inc(settled, 1)
                with dve.Fori(0, 4 * KT // 2) as r:
                    for b in range(2):
                        dve.wait_ge(piece_done, upto(l, piece_done, r * 2 + (Q_GATE + b + 1)))
                        V.tensor_scalar(gates[:, bass.ds(r * 2 + b, 1), :], ps[:, b:b + 1, 0:T],
                                        vec[:, bass.ds(r * 2 + (V_GATE + b), 1)], None, ALU.add).then_inc(bank_free[b], 1)

                def merged_low(m):
                    dve.wait_ge(merged_h, upto(l, merged_h, m + 1))
                    V.tensor_tensor(hl[:, m, :], work[:, m, :], hh[:, m, :].bitcast(F32), ALU.subtract).then_inc(merged_l, 1)

                for t in range(4 * KT):
                    b, m, k = t // KT, t % KT, t % 2
                    dve.wait_ge(piece_done, upto(l, piece_done, Q_BRANCH + t + 1))
                    if m == 0:
                        dve.wait_ge(sigmoid_ready, upto(l, sigmoid_ready, b + 1))
                    if b == 0:
                        V.tensor_tensor(work[:, m, :], ps[:, k, 0:T], gates[:, t, :], ALU.mult).then_inc(bank_free[k], 1)
                    else:
                        V.tensor_tensor(gates[:, t, :], ps[:, k, 0:T], gates[:, t, :], ALU.mult).then_inc(bank_free[k], 1)
                        dve.wait_ge(bank_free[k], taken(l, (NIN + 4 * KT + t) // 2 + 1))
                        i = V.tensor_tensor(work[:, m, :], work[:, m, :], gates[:, t, :], ALU.add)
                        if b == 3:
                            i.then_inc(merged, 1)
                            if m >= 4:
                                merged_low(m - 4)
                for m in range(KT - 4, KT):
                    merged_low(m)

                def add_out(m, bank, gate_at, cols, group_inc):
                    for g, ((a, b), c) in enumerate(zip(((0, TP), (TP, T)), cols)):
                        i = V.scalar_tensor_tensor(x[:, m, a:b], ps[:, bank, c:c + b - a], mod[:, gate_at + m, g:g + 1],
                                                   x[:, m, a:b], ALU.mult, ALU.add)
                    i.then_inc(bank_free[bank], 1)

                for m in range(KT):
                    dve.wait_ge(piece_done, upto(l, piece_done, done(Q_OUT + m)))
                    add_out(m, m % 2, 16, (0, TP), None)
                dve.wait_ge(bank_free[0], taken(l, (NIN + 9 * KT) // 2))
                dve.wait_ge(bank_free[1], taken(l, (NIN + 9 * KT) // 2))
                norm(2)

                dve.wait_ge(tail_stored, upto(l, tail_stored, 0))
                in_order(V.memset(up[:, :, 0:2], 0.0))

                def convolve(p, odd, first):
                    for g in range(2):
                        u = 2 * odd + g
                        at = (lambda base, n=1: bass.ds(p + base, n)) if not isinstance(p, int) else \
                            (lambda base, n=1: slice(p + base, p + base + n))
                        at2 = (lambda base: bass.ds(p * 2 + base, 2)) if not isinstance(p, int) else \
                            (lambda base: slice(p * 2 + base, p * 2 + base + 2))
                        w = [vec[:, at(V_CONV + j * 2 * FT + g * FT)] for j in range(3)]
                        cb = vec[:, at(V_CB + g * FT)]
                        k = 0 if first else 2
                        dve.wait_ge(up_copied, upto(l, up_copied, p * 2 + (g + 1)))
                        conv_link(V.tensor_copy(up[:, u, 2 + TP:4 + TP], vec[:, at2(V_ST + 2 * g * FT)]))
                        conv_link(V.tensor_scalar(conv[:, u, :], up[:, u, 0:CC], w[0], cb, ALU.mult, ALU.add))
                        conv_link(V.scalar_tensor_tensor(conv[:, u, :], up[:, u, 1:1 + CC], w[1], conv[:, u, :], ALU.mult, ALU.add))
                        V.tensor_copy(tail[:, at(g * FT), 0:2], up[:, u:u + 1, TP:TP + 2])
                        V.tensor_copy(tail[:, at(g * FT), 2:4], up[:, u:u + 1, UC - 2:UC])
                        V.scalar_tensor_tensor(conv[:, u, :], up[:, u, 2:2 + CC], w[2], conv[:, u, :], ALU.mult, ALU.add).then_inc(convolved, 1)

                def multiply(p, odd):
                    dve.wait_ge(silued, upto(l, silued, p + 1))
                    if not isinstance(p, int) or p >= 2:
                        dve.wait_ge(fal_ready, upto(l, fal_ready, p - 1))
                    dve.wait_ge(convolved, upto(l, convolved, p * 2 + 2))
                    V.tensor_tensor(prod[:, odd, :], sil[:, odd, :], conv[:, 2 * odd + 1, :], ALU.mult).then_inc(product_ready, 1)

                def product_low(p, odd):
                    dve.wait_ge(fah_ready, upto(l, fah_ready, p + 1))
                    o = (bass.ds(p, 1) if not isinstance(p, int) else slice(p, p + 1))
                    V.tensor_tensor(fal[:, o, :], prod[:, odd:odd + 1, :], fah[:, o, :].bitcast(F32), ALU.subtract).then_inc(fal_ready, 1)

                def conv_link(ins):
                    in_order(ins, conv_at[0])

                conv_at = [0]
                convolve(0, 0, True)
                convolve(1, 1, True)
                multiply(0, 0)
                with dve.Fori(0, FT // 2 - 1) as r:
                    conv_at[0] = r * CONV_LINKS
                    before = count[0]
                    for odd in range(2):
                        convolve(r * 2 + (2 + odd), odd, False)
                        product_low(r * 2 + odd, odd)
                        multiply(r * 2 + (1 + odd), 1 - odd)
                    assert count[0] - before == CONV_LINKS, count[0] - before
                count[0] += CONV_LINKS * (FT // 2 - 2)
                conv_at[0] = 0
                product_low(FT - 2, 0)
                multiply(FT - 1, 1)
                product_low(FT - 1, 1)

                with dve.Fori(0, 4) as r:
                    for b in range(2):
                        dve.wait_ge(piece_done, upto(l, piece_done, r * 6 + (done(Q_DOWN + 2) + 3 * b)))
                        for g, (a, n, c) in enumerate(((0, TP, 0), (TP, TS, TP + 2))):
                            i = V.scalar_tensor_tensor(
                                x[:, bass.ds(r * 2 + b, 1), a:a + n], ps[:, b:b + 1, c:c + n],
                                mod[:, bass.ds(r * 2 + (40 + b), 1), g],
                                x[:, bass.ds(r * 2 + b, 1), a:a + n], ALU.mult, ALU.add)
                        i.then_inc(bank_free[b], 1)
                dve.wait_ge(bank_free[0], taken(l, (2 * TILES2) // 2))
                dve.wait_ge(bank_free[1], taken(l, (2 * TILES2) // 2))
                assert count[0] == DVE_LINKS, ("DVE_LINKS", count[0])

            dve.wait_ge(fin[3], 1)
            count = [0]

            def link(ins):
                count[0] += 1
                ins.then_inc(fin[4], 1)
                dve.wait_ge(fin[4], count[0])

            newton(link, DM)
            for k in range(KT):
                V.scalar_tensor_tensor(work[:, k, :], x[:, k, :], fg[:, k:k + 1], rstd[:, 0, :], ALU.mult, ALU.mult).then_inc(y_ready, 1)


CONV_LINKS = 12
LINKS = (15, 245)


_OUTS = [("y_fm", (P, KT, T)), ("o_proj", (DEPTH, 6, P, 2, T)), ("o_ki", (DEPTH, IDX, T)), ("o_vb", (DEPTH, 2, P, TS)),
         ("o_logf", (DEPTH, NH, T)), ("o_conv", (DEPTH, P, 2 * FT, 4))]


def _constants(np):
    c = np.zeros((P, NCONST), np.float32)
    i, j = np.arange(P)[:, None], np.arange(P)[None, :]
    c[:, C_ID:C_ID + P] = i == j
    for at, width in ((C_PA, HD), (C_PI, IDX)):
        half = width // 2
        partner = j // width * width + (j % width + half) % width
        c[:, at:at + P] = i == partner
    c[:, C_ADM:C_ADM + P] = np.where((i < 64) & (j >= 64), INADMISSIBLE, 0)
    c[:, C_CAUSAL:C_CAUSAL + P] = np.where(j <= i, 0, MASKED)
    c[:, C_STRICT:C_STRICT + P] = np.where(i < j, 0, MASKED)
    c[:, C_STRICT1:C_STRICT1 + P] = i < j
    c[:, C_SPAT:C_SPAT + P] = i <= j
    c[:, C_NTRI:C_NTRI + P] = -(i >= j).astype(np.float32)
    c[:, C_NONE:C_NONE + P] = -1
    c[:, C_ONE:C_ONE + P] = 1
    c[0:TS, C_REP:C_REP + P] = (np.arange(TS)[:, None] == j % TS)
    pos = np.concatenate([np.arange(TP), PAST + np.arange(TS)]).astype(np.float32)
    for width, cos_at, sin_at in ((HD, C_COSA, C_SINA), (IDX, C_COSI, C_SINI)):
        half = width // 2
        inv = np.float32(10000.0) ** (-np.arange(half, dtype=np.float32) / np.float32(half))
        ang = inv[np.arange(P) % half][:, None] * pos[None, :]
        c[:, cos_at:cos_at + T] = np.cos(ang)
        c[:, sin_at:sin_at + T] = np.sin(ang) * np.where(np.arange(P) % width < half, -1, 1)[:, None]
    c[:, C_NEW:C_NEW + TS] = np.where(np.arange(TS)[None, :] <= np.arange(P)[:, None] % TS, 0, MASKED)
    c[:, C_QS:C_QS + NIN] = 1
    for t in (AQ, CQ, DQ):
        c[:, C_QS + t:C_QS + t + 2] = HD ** -0.5
    c[WROW:WROW + IH, C_QS + MISC] = (IDX * IH) ** -0.5
    c[:, C_EPS] = EPS
    c[4:8, C_FR], c[0:4, C_FR + 1] = 1, 1
    for h in range(NH):
        c[h, C_FL + 2 * h], c[4 + h, C_FL + 2 * h + 1] = 1, -1
    c[0:HD, C_HALF], c[HD:, C_HALF + 1] = 1, 1
    return c


def _layout(np, a):
    def fm(v):
        v = v.reshape(*v.shape[:-1], v.shape[-1] // P, P)
        return np.moveaxis(v, -1, 0)

    out = {}
    tokens = np.concatenate([a["x_prompt"][0], a["x_sample"][0]])
    out["x_fm"] = fm(tokens).transpose(0, 2, 1)
    mod = np.stack([w.reshape(4, 2, P, MOD_BLOCKS, 512).transpose(3, 0, 2, 1, 4).reshape(NMOD, P, PIECE)
                    for w in a["w_mod"]])
    out["mod_first"] = mod[0, :MOD_A]
    out["mod_vecs"] = np.stack([np.concatenate([fm(a["b_mod"][l]), fm(a["norm1_g"][l]), fm(a["norm2_g"][l])], axis=1)
                                for l in (*range(DEPTH), 0)], axis=1).reshape(P, -1)
    out["c_fm"] = fm(np.concatenate([a["c_prompt"], a["c_sample"]])).transpose(0, 2, 1)
    stream = np.zeros((DEPTH, NPIECE, P, PIECE), np.float32)

    def tiles_of(w):
        n = w.shape[1] // P
        return w.reshape(KT, P, n, P).transpose(2, 1, 0, 3).reshape(n, P, DM)

    widths = [256, 256, 256, 256, 32, 8, 256, 256, 256, 256, 256, 4, 256, 256, 256]
    at = np.concatenate([[0], np.cumsum(widths)])
    vecs = np.zeros((DEPTH, P, NVEC), np.float32)
    for l in range(DEPTH):
        (q, k, v, qi, ki, w, bu, bv, cq, ck, cv, cf, dq, dk, dv) = (
            a["w_in"][l][:, at[i]:at[i + 1]] for i in range(len(widths)))
        misc = np.zeros((DM, P), np.float32)
        misc[:, FROW:FROW + 4] = cf
        misc[:, FROW + 4:FROW + 8] = cf
        misc[:, WROW:WROW + IH] = w
        w_in = np.concatenate([qi, ki, ki, ki, ki, misc, bu, bv, dq, dk, dv, q, k, v, cq, ck, cv], axis=1)
        s = np.zeros((NSPLIT, P, PIECE), np.float32)
        s[Q_IN:Q_GATE] = tiles_of(w_in)
        s[Q_GATE:Q_BRANCH] = tiles_of(a["w_gate"][l])
        s[Q_BRANCH:Q_OUT] = a["w_branch"][l].reshape(4, 2, P, 2, 512).transpose(0, 3, 2, 1, 4).reshape(8, P, PIECE)
        s[Q_OUT:Q_UP] = tiles_of(a["w_out"][l])
        s[Q_UP:Q_DOWN].reshape(FT, 2, P, PIECE)[:, 0] = tiles_of(a["w_up"][l][:, :FF])
        s[Q_UP:Q_DOWN].reshape(FT, 2, P, PIECE)[:, 1] = tiles_of(a["w_up"][l][:, FF:])
        down = a["w_down"][l].reshape(FT, P, KT, P).transpose(2, 1, 0, 3)
        k0 = 0
        for c, n in enumerate(DOWN_SPLIT):
            s[Q_DOWN + c::3][:, :, :n * P] = down[:, :, k0:k0 + n].reshape(KT, P, n * P)
            k0 += n
        stream[l] = np.concatenate([s[:NIN], mod[l, MOD_A:], mod[(l + 1) % DEPTH, :MOD_A], s[NIN:]])
        v = vecs[l]
        v[:, V_LG:V_LG + 2] = fm(a["lnv_g"][l])
        v[:, V_LB:V_LB + 2] = fm(a["lnv_b"][l])
        v[:, V_GATE:V_GATE + 4 * KT] = fm(a["b_gate"][l])
        v[:, V_CONV:V_CB] = fm(a["w_conv"][l]).reshape(P, -1)
        v[:, V_CB:V_ST] = fm(a["b_conv"][l])
        v[:, V_ST:V_FB] = fm(a["state_ffn_conv"][l, 0]).transpose(0, 2, 1).reshape(P, -1)
        v[0:4, V_FB] = a["f_bias"][l]
        v[4:8, V_FB] = a["f_bias"][l]
        v[:, V_BS:V_BS + 2 * P] = np.repeat(a["b_spatial"][l].reshape(2, 2, P).transpose(1, 0, 2), 64, axis=0).reshape(P, 2 * P)
    out["stream"], out["vecs"], out["consts"] = stream, vecs, _constants(np)
    out["final_g"] = fm(a["final_g"])
    keys = np.stack([a["cache_a_k"], a["cache_c_k"], a["cache_d_k"]], axis=1)[:, :, 0]
    out["keys_t"] = keys.reshape(DEPTH, 3, PAST, 2, P).transpose(0, 1, 4, 3, 2)
    vals = np.stack([a["cache_a_v"], a["cache_c_v"], a["cache_d_v"]], axis=1)[:, :, 0]
    out["vals"] = vals.reshape(DEPTH, 3, 4, P, 256).transpose(0, 1, 3, 2, 4)
    ki_t = a["cache_a_kidx"][:, 0].transpose(0, 2, 1)
    out["kidx_t"] = np.concatenate([ki_t] * 4, axis=1)
    lp = a["cache_c_logf"][:, 0].transpose(0, 2, 1)
    out["logf_past"] = np.concatenate([lp, lp], axis=1)
    out["w_sp_t"] = a["w_spatial"].transpose(0, 3, 1, 2)
    return {k: np.ascontiguousarray(v) for k, v in out.items()}


def kernel(**inputs):
    import numpy as np
    import concourse.bacc as bacc
    from concourse.bass_utils import run_bass_kernel_spmd

    a = _layout(np, {k: np.asarray(v) for k, v in inputs.items()})
    nc = bacc.Bacc("TRN2", target_bir_lowering=False, num_devices=1)
    args = [nc.dram_tensor(k, v.shape, mybir.dt.from_np(v.dtype), kind="ExternalInput").ap() for k, v in a.items()]
    args += [nc.dram_tensor(n, shape, F32, kind="ExternalOutput").ap() for n, shape in _OUTS]
    encoder(nc, *args)
    r = run_bass_kernel_spmd(nc, [a], core_ids=[0]).results[0]

    y = r["y_fm"].transpose(2, 1, 0).reshape(T, DM)
    rows = r["o_proj"].transpose(1, 0, 4, 3, 2).reshape(6, DEPTH, T, NH, HD)
    split = lambda v: (np.ascontiguousarray(v[:, None, :TP]), np.ascontiguousarray(v[:, None, TP:]))
    ki = split(r["o_ki"].transpose(0, 2, 1))
    lf = split(r["o_logf"].transpose(0, 2, 1))
    vb = np.ascontiguousarray(r["o_vb"].transpose(0, 3, 1, 2).reshape(DEPTH, 1, TS, 2 * P))
    conv = r["o_conv"].transpose(0, 3, 2, 1).reshape(DEPTH, 1, 4, 2 * FF)
    ak, av, ck, cv, dk, dv = (split(rows[i]) for i in range(6))
    return (np.ascontiguousarray(y[None, :TP]), np.ascontiguousarray(y[None, TP:]), *ak, *av, *ki, vb, *ck, *cv, *lf, *dk, *dv,
            np.ascontiguousarray(conv[:, :, 0:2]), np.ascontiguousarray(conv[:, :, 2:4]))
```
